# Optimizing a Trainium2 kernel written in Bass

```python
import math
import jax, jax.numpy as jnp
from jax import lax
import numpy as np

D_MODEL = 1024
BATCH = 1
SEQ = 256
DEPTH = 2

MEM_LEN = 256
Q_BLOCK = 128
RMS_EPS = 1e-6
SSM_WIDTH = D_MODEL // 2
SSM_GROUP = 16
SSM_GROUPS = SSM_WIDTH // SSM_GROUP
SSM_STATE = 64
SB_HEADS = 8
SB_HEAD_DIM = 64
SB_WIDTH = SB_HEADS * SB_HEAD_DIM
DA_HEADS = 4
DA_QK_DIM = 64
DA_V_DIM = 2 * DA_QK_DIM
DA_QK_WIDTH = DA_HEADS * 2 * DA_QK_DIM
DA_WIDTH = DA_HEADS * DA_V_DIM
ROT_DIM = DA_QK_DIM // 4
ROPE_THETA = 500000.0
N_BRANCH = 3
BRANCH_WIDTH = 512
XA_HEADS = 4
XA_HEAD_DIM = 128
XA_WIDTH = XA_HEADS * XA_HEAD_DIM
MLP_HIDDEN = 4 * D_MODEL
IN_SPLITS = (SSM_WIDTH, SB_WIDTH, SB_WIDTH, SB_WIDTH, DA_QK_WIDTH, DA_QK_WIDTH, DA_WIDTH, N_BRANCH * D_MODEL)
N_IN = sum(IN_SPLITS)

kernel_name = 'hybrid_s5_stickbreak_diffattn_gated'

def rmsnorm(x, gain):
    x32 = x.astype(jnp.float32)
    y = x32 * lax.rsqrt(jnp.mean(x32 * x32, axis=-1, keepdims=True) + RMS_EPS)
    return (y * gain.astype(jnp.float32)).astype(x.dtype)

def rope_partial(t, cos, sin):
    half = ROT_DIM // 2
    t1 = t[..., :half]
    t2 = t[..., half:ROT_DIM]
    return jnp.concatenate([t1 * cos - t2 * sin, t2 * cos + t1 * sin, t[..., ROT_DIM:]], axis=-1)

def query_blocks(fn, q):
    b, h, s, d = q.shape
    nb = s // Q_BLOCK
    qb = q.reshape(b, h, nb, Q_BLOCK, d).transpose(2, 0, 1, 3, 4)
    starts = jnp.arange(nb, dtype=jnp.int32) * Q_BLOCK
    out = lax.map(lambda a: fn(a[0], a[1]), (qb, starts))
    return out.transpose(1, 2, 0, 3, 4).reshape(b, h, s, out.shape[-1])

def stick_breaking_attention(q, k, v):
    scale = q.shape[-1] ** -0.5
    key_idx = jnp.arange(k.shape[2])

    def blk(qb, t0):
        q_idx = t0 + jnp.arange(Q_BLOCK)
        mask = key_idx[None, :] < q_idx[:, None]
        z = jnp.einsum('bhqd,bhkd->bhqk', qb, k).astype(jnp.float32) * scale
        log_1mb = jnp.where(mask, jax.nn.log_sigmoid(-z), 0.0)
        later = lax.cumsum(log_1mb, axis=3, reverse=True) - log_1mb
        w = jnp.where(mask, jnp.exp(jax.nn.log_sigmoid(z) + later), 0.0)
        return jnp.einsum('bhqk,bhkd->bhqd', w.astype(v.dtype), v)

    return query_blocks(blk, q)

def differential_attention(q, k, v, lam):
    dk = q.shape[-1] // 2
    scale = dk ** -0.5
    k1 = k[..., :dk]
    k2 = k[..., dk:]
    key_idx = jnp.arange(k.shape[2])

    def blk(qb, t0):
        q_idx = t0 + jnp.arange(Q_BLOCK)
        mask = key_idx[None, :] <= q_idx[:, None]
        s1 = jnp.einsum('bhqd,bhkd->bhqk', qb[..., :dk], k1).astype(jnp.float32) * scale
        s2 = jnp.einsum('bhqd,bhkd->bhqk', qb[..., dk:], k2).astype(jnp.float32) * scale
        p1 = jax.nn.softmax(jnp.where(mask, s1, -jnp.inf), axis=-1)
        p2 = jax.nn.softmax(jnp.where(mask, s2, -jnp.inf), axis=-1)
        w = p1 - lam * p2
        return jnp.einsum('bhqk,bhkd->bhqd', w.astype(v.dtype), v)

    return query_blocks(blk, q)

def _ssm_combine(e1, e2):
    a1, b1 = e1
    a2, b2 = e2
    return a2 * a1, a2 * b1 + b2

def s5_ssm(u, lam_re, lam_im, log_dt, b_re, b_im, c_re, c_im, d_skip):
    bsz, seq, _ = u.shape
    ug = u.astype(jnp.float32).reshape(bsz, seq, SSM_GROUPS, SSM_GROUP)
    lam = lax.complex(lam_re.astype(jnp.float32), lam_im.astype(jnp.float32))
    dt = jnp.exp(log_dt.astype(jnp.float32))[:, None]
    lam_bar = jnp.exp(lam * dt)
    bmat = lax.complex(b_re.astype(jnp.float32), b_im.astype(jnp.float32))
    b_bar = ((lam_bar - 1.0) / lam)[..., None] * bmat
    bu = jnp.einsum('gpc,blgc->blgp', b_bar, ug.astype(jnp.complex64))
    a = jnp.broadcast_to(lam_bar, bu.shape)
    _, states = lax.associative_scan(_ssm_combine, (a, bu), axis=1)
    y = (jnp.einsum('gcp,blgp->blgc', c_re.astype(jnp.float32), states.real)
         - jnp.einsum('gcp,blgp->blgc', c_im.astype(jnp.float32), states.imag))
    y = y + d_skip.astype(jnp.float32).reshape(SSM_GROUPS, SSM_GROUP) * ug
    return y.reshape(bsz, seq, SSM_WIDTH).astype(u.dtype)

def _normal(k, shape, scale):
    return jax.random.normal(k, shape, jnp.float32) * scale

def setup_inputs(seed: int = 0) -> dict:
    key = jax.random.key(seed)
    ks = jax.random.split(key, 32)
    gain = lambda k, shape: 1.0 + _normal(k, shape, 0.02)
    offsets = jax.random.randint(ks[2], (BATCH, 1), 0, 1024, dtype=jnp.int32)
    positions = offsets + jnp.arange(SEQ, dtype=jnp.int32)[None, :]
    lam_im = jnp.pi * jnp.arange(SSM_STATE, dtype=jnp.float32)[None, None, :] + _normal(ks[7], (DEPTH, SSM_GROUPS, SSM_STATE), 0.01)
    return {
        'x': _normal(ks[0], (BATCH, SEQ, D_MODEL), 1.0),
        'mem': _normal(ks[1], (BATCH, MEM_LEN, D_MODEL), 1.0),
        'positions': positions,
        'norm_mix': gain(ks[3], (DEPTH, D_MODEL)),
        'w_in': _normal(ks[4], (DEPTH, D_MODEL, N_IN), D_MODEL ** -0.5),
        'ssm_lam_re': -0.5 + _normal(ks[6], (DEPTH, SSM_GROUPS, SSM_STATE), 0.01),
        'ssm_lam_im': lam_im,
        'ssm_log_dt': jax.random.uniform(ks[8], (DEPTH, SSM_GROUPS), jnp.float32, math.log(1e-3), math.log(1e-1)),
        'ssm_b_re': _normal(ks[9], (DEPTH, SSM_GROUPS, SSM_STATE, SSM_GROUP), (2 * SSM_GROUP) ** -0.5),
        'ssm_b_im': _normal(ks[10], (DEPTH, SSM_GROUPS, SSM_STATE, SSM_GROUP), (2 * SSM_GROUP) ** -0.5),
        'ssm_c_re': _normal(ks[11], (DEPTH, SSM_GROUPS, SSM_GROUP, SSM_STATE), (2 * SSM_STATE) ** -0.5),
        'ssm_c_im': _normal(ks[12], (DEPTH, SSM_GROUPS, SSM_GROUP, SSM_STATE), (2 * SSM_STATE) ** -0.5),
        'ssm_d': _normal(ks[13], (DEPTH, SSM_WIDTH), 1.0),
        'ssm_w_glu': _normal(ks[14], (DEPTH, SSM_WIDTH, 2 * SSM_WIDTH), SSM_WIDTH ** -0.5),
        'diff_lambda': _normal(ks[15], (DEPTH, 4, DA_QK_DIM), 0.1),
        'diff_subln': gain(ks[16], (DEPTH, DA_V_DIM)),
        'w_branch': _normal(ks[17], (DEPTH, N_BRANCH, BRANCH_WIDTH, D_MODEL), BRANCH_WIDTH ** -0.5),
        'w_out': _normal(ks[18], (DEPTH, D_MODEL, D_MODEL), D_MODEL ** -0.5),
        'norm_cross': gain(ks[19], (DEPTH, D_MODEL)),
        'norm_mem': gain(ks[20], (DEPTH, D_MODEL)),
        'w_xq': _normal(ks[21], (DEPTH, D_MODEL, XA_WIDTH), D_MODEL ** -0.5),
        'w_xkv': _normal(ks[22], (DEPTH, D_MODEL, 2 * XA_WIDTH), D_MODEL ** -0.5),
        'w_xo': _normal(ks[23], (DEPTH, XA_WIDTH, D_MODEL), XA_WIDTH ** -0.5),
        'norm_mlp': gain(ks[24], (DEPTH, D_MODEL)),
        'w_up': _normal(ks[25], (DEPTH, D_MODEL, MLP_HIDDEN), D_MODEL ** -0.5),
        'w_down': _normal(ks[26], (DEPTH, MLP_HIDDEN, D_MODEL), MLP_HIDDEN ** -0.5),
        'norm_final': gain(ks[27], (D_MODEL,)),
    }

def reference(x, mem, positions, norm_mix, w_in, ssm_lam_re, ssm_lam_im, ssm_log_dt, ssm_b_re, ssm_b_im,
              ssm_c_re, ssm_c_im, ssm_d, ssm_w_glu, diff_lambda, diff_subln, w_branch, w_out,
              norm_cross, norm_mem, w_xq, w_xkv, w_xo, norm_mlp, w_up, w_down, norm_final):
    bsz, seq, _ = x.shape
    split_idx = np.cumsum(IN_SPLITS)[:-1].tolist()

    inv_freq = ROPE_THETA ** (-jnp.arange(0, ROT_DIM, 2, dtype=jnp.float32) / ROT_DIM)
    ang = positions.astype(jnp.float32)[..., None] * inv_freq
    cos = jnp.cos(ang)[:, :, None, None, :].astype(x.dtype)
    sin = jnp.sin(ang)[:, :, None, None, :].astype(x.dtype)

    def heads(t, n):
        return t.reshape(bsz, seq, n, -1).transpose(0, 2, 1, 3)

    def merge_heads(t):
        return t.transpose(0, 2, 1, 3).reshape(bsz, seq, -1)

    for l in range(DEPTH):
        h = rmsnorm(x, norm_mix[l])
        u, sq, sk, sv, dq, dk, dv, gate_logits = jnp.split(h @ w_in[l], split_idx, axis=-1)

        y_ssm = jax.nn.gelu(s5_ssm(u, ssm_lam_re[l], ssm_lam_im[l], ssm_log_dt[l], ssm_b_re[l], ssm_b_im[l],
                                   ssm_c_re[l], ssm_c_im[l], ssm_d[l]))
        glu_a, glu_b = jnp.split(y_ssm @ ssm_w_glu[l], 2, axis=-1)
        y_ssm = glu_a * jax.nn.sigmoid(glu_b)

        y_sb = merge_heads(stick_breaking_attention(heads(sq, SB_HEADS), heads(sk, SB_HEADS), heads(sv, SB_HEADS)))

        dq_r = rope_partial(dq.reshape(bsz, seq, DA_HEADS, 2, DA_QK_DIM), cos, sin)
        dk_r = rope_partial(dk.reshape(bsz, seq, DA_HEADS, 2, DA_QK_DIM), cos, sin)
        dq_r = dq_r.reshape(bsz, seq, DA_HEADS, 2 * DA_QK_DIM).transpose(0, 2, 1, 3)
        dk_r = dk_r.reshape(bsz, seq, DA_HEADS, 2 * DA_QK_DIM).transpose(0, 2, 1, 3)
        lam_vec = diff_lambda[l].astype(jnp.float32)
        lam_init = 0.8 - 0.6 * math.exp(-0.3 * l)
        lam = (jnp.exp(jnp.sum(lam_vec[0] * lam_vec[1])) - jnp.exp(jnp.sum(lam_vec[2] * lam_vec[3]))
               + lam_init)
        o = differential_attention(dq_r, dk_r, heads(dv, DA_HEADS), lam)
        o = rmsnorm(o, diff_subln[l]) * (1.0 - lam_init)
        y_da = merge_heads(o)

        branches = jnp.stack([y_ssm, y_sb, y_da], axis=2)
        proj = jnp.einsum('bsnc,ncd->bsnd', branches, w_branch[l])
        gates = jax.nn.sigmoid(gate_logits.reshape(bsz, seq, N_BRANCH, D_MODEL))
        x = x + jnp.sum(gates * proj, axis=2) @ w_out[l]

        hx = rmsnorm(x, norm_cross[l])
        m = rmsnorm(mem, norm_mem[l])
        xq = hx.reshape(bsz, seq, D_MODEL) @ w_xq[l]
        xq = xq.reshape(bsz, seq, XA_HEADS, XA_HEAD_DIM)
        xk, xv = jnp.split(m @ w_xkv[l], 2, axis=-1)
        xk = xk.reshape(bsz, -1, XA_HEADS, XA_HEAD_DIM)
        xv = xv.reshape(bsz, -1, XA_HEADS, XA_HEAD_DIM)
        sc = jnp.einsum('bshd,bmhd->bhsm', xq, xk).astype(jnp.float32) * (XA_HEAD_DIM ** -0.5)
        p = jax.nn.softmax(sc, axis=-1).astype(xv.dtype)
        xo = jnp.einsum('bhsm,bmhd->bshd', p, xv).reshape(bsz, seq, XA_WIDTH)
        x = x + xo @ w_xo[l]

        hm = rmsnorm(x, norm_mlp[l])
        x = x + jnp.square(jax.nn.relu(hm @ w_up[l])) @ w_down[l]

    return rmsnorm(x, norm_final)


_drawn_inputs = setup_inputs


def setup_inputs(seed=0):
    import zlib

    import numpy as np

    out = dict(_drawn_inputs(seed))
    spreads = {}
    factors = {'norm_mix': 2.967,
     'ssm_lam_re': 64.0,
     'ssm_lam_im': 37.056,
     'ssm_log_dt': 32.088,
     'ssm_b_re': 49.992,
     'ssm_b_im': 42.546,
     'ssm_c_re': 34.632,
     'ssm_c_im': 46.313,
     'diff_lambda': 7.74,
     'diff_subln': 5.585,
     'norm_cross': 8.0,
     'norm_mem': 8.0,
     'norm_final': 9.657}
    for name, (base, spread) in spreads.items():
        noise = np.random.default_rng([zlib.crc32(name.encode()), seed]).standard_normal(out[name].shape)
        drawn = base * np.exp(spread * noise) if base else spread * noise
        out[name] = __import__('jax').numpy.asarray(drawn.astype(out[name].dtype))
    for name, factor in factors.items():
        out[name] = (out[name] * factor).astype(out[name].dtype)
    return out
```

```python
import math
from contextlib import ExitStack

import numpy as np

import concourse.bass as bass
from concourse import mybir

ALU = mybir.AluOpType
ACT = mybir.ActivationFunctionType
AX = mybir.AxisListType
F32 = mybir.dt.float32
F32R = mybir.dt.float32r
I32 = mybir.dt.int32

P = 128
DEPTH, D, T = 2, 1024, 256
NT = T // P
KD = D // P
BW = 512
KB = BW // P
HIDDEN = 4 * D
SB_HEADS, HD = 8, 64
DA_HEADS = 4
XA_HEADS = 4
ROT, ROT_HALF = 16, 8
ROPE_THETA = 500000.0
RMS_EPS = 1e-6
GROUPS, GC, STATES = 32, 16, 64
STILES = GROUPS * STATES // P
SSM_STEPS = STILES // 2
BIG, NEG = 3.0e38, -1.0e30
TWO_PI = 2 * math.pi
PI_HI = float(np.float32(6.28125))
PI_MID = float(np.float32(TWO_PI - 6.28125))
PI_LO = float(np.float32(TWO_PI - 6.28125 - float(np.float32(TWO_PI - 6.28125))))
PI_SAFE = float(np.nextafter(np.float32(math.pi), np.float32(0)))
ROUND = 1.5 * 2.0 ** 23

UW = 2048
RAW, HL = 3, 2
POOL_COLS = 768

R_MIX, R_CROSS, R_MEM, R_MLP, R_D, R_SUBLN, R_LRE, R_LIM, R_DT, R_END = 0, 8, 16, 24, 32, 36, 37, 53, 96, 112


def plan():
    units, name = [], {}

    def add(key, *u):
        name[key] = len(units)
        units.append(u)

    def wide(key, mat, kind, c0, n=2):
        for i in range(n):
            if kind == "T":
                add((key, i), mat, "T", KD, 256, 0, c0 + 256 * i)
            else:
                add((key, i), mat, "N", 4, 512, 4 * (i % 2), c0 + 512 * (i // 2))

    wide("u", "w_in", "T", 0)
    wide("sq", "w_in", "T", 512)
    wide("sk", "w_in", "T", 1024)
    wide("sv", "w_in", "N", 1536)
    wide("dq", "w_in", "N", 2048)
    wide("dk", "w_in", "N", 2560)
    wide("dv", "w_in", "N", 3072)
    for n in (1, 2, 0):
        wide(("gate", n), "w_in", "T", 3584 + D * n, 4)
    add(("glu", 1), "ssm_w_glu", "T", KB, 512, 0, 512)
    add(("glu", 0), "ssm_w_glu", "T", KB, 512, 0, 0)
    for cb in range(2):
        for n in (1, 2, 0):
            add(("branch", cb, n), ("w_branch", n), "T", KB, 512, 0, 512 * cb)
    wide("wout", "w_out", "N", 0, 4)
    wide("xk", "w_xkv", "T", 0)
    wide("xq", "w_xq", "T", 0)
    wide("xv", "w_xkv", "N", BW)
    for cb in range(2):
        add(("xo", cb), "w_xo", "N", 4, 512, 0, 512 * cb)

    def up(g):
        for i in range(2):
            add(("up", g, i), "w_up", "T", KD, 256, 0, 512 * g + 256 * i)

    def down(g):
        for cb in range(2):
            add(("down", g, cb), "w_down", "N", 4, 512, 4 * g, 512 * cb)

    groups = HIDDEN // 512
    up(0)
    for g in range(1, groups):
        up(g)
        down(g - 1)
    down(groups - 1)
    return units, name


UNITS, AT_UNIT = plan()
NU = len(UNITS)
assert NU % RAW == 0 and NU % HL == 0


def side_stages():
    side = {u: [] for u in range(-1, NU)}

    def after(u, *stage):
        side[u].append(stage)

    after(-1, "params")
    after(-1, "stats", "mix", 0)
    after(-1, "stats", "mix", 1)
    after(-1, "norm", "mix")
    after(0, "ssm_prep")
    for k in range(8):
        after(1 + k // 2, "ssm_pow", k)
    after(3, "ssm_ct")
    after(4, "ssm_bt")
    for h in range(SB_HEADS):
        after(6 + h, "sb_s", h)
        after(7 + h, "sb_u", h)
        after(8 + h, "sb_p", h)
    after(10, "rope", 0)
    after(11, "turn", 0)
    after(12, "rope", 1)
    after(13, "turn", 1)
    for i in range(SSM_STEPS):
        after(7 + 2 * i, "ssm_in", i)
        after(8 + 2 * i, "ssm_rot", i)
        after(9 + 2 * i, "ssm_out", i)
    after(24, "gelu")
    for j in range(2 * DA_HEADS):
        after(16 + j, "da_s", j)
        after(17 + j, "da_t", j)
        after(18 + j, "da_p", j)
    after(21, "da_n", 0)
    after(22, "da_o", 0)
    after(25, "da_n", 1)
    after(26, "da_o", 1)
    after(33, "memg")
    after(AT_UNIT["wout", 1], "stats", "cross", 0)
    after(AT_UNIT["wout", 3], "stats", "cross", 1)
    after(AT_UNIT["xk", 1], "norm", "cross")
    xq = AT_UNIT["xq", 0]
    for h in range(XA_HEADS):
        after(xq + h // 2, "xa_s", h)
        after(xq + 1 + (h + 1) // 2, "xa_t", h)
    for h in range(XA_HEADS):
        after(xq + 3, "xa_p", h)
    after(AT_UNIT["xo", 0], "stats", "mlp", 0)
    after(AT_UNIT["xo", 1], "stats", "mlp", 1)
    after(AT_UNIT["xo", 1], "norm", "mlp")
    return side


SIDE = side_stages()
STAGES_FIRST = set(range(6, 28)) | set(range(AT_UNIT["xq", 0], AT_UNIT["xo", 0]))
_RANK = {"sb_p": 0, "da_p": 0, "sb_u": 1, "da_t": 1, "sb_s": 2, "da_s": 2, "da_o": -1, "da_n": 3, "ssm_in": 4, "ssm_rot": 5,
         "ssm_out": 6}
for _u in range(7, 27):
    SIDE[_u].sort(key=lambda s: _RANK.get(s[0], 7))


def unit_banks(key):
    if key[0] in ("u", "sq", "sk", "xk", "xq") or isinstance(key[0], tuple):
        return ["T0", "T1"][key[1] % 2:][:1]
    if key[0] in ("sv", "dq", "dk", "dv", "xv"):
        return ["T0", "T1"]
    if key[0] == "glu":
        return ["T0", "T1"] if key[1] else ["A0", "A1"]
    if key[0] == "branch":
        return {1: ["T0", "T1"], 2: ["A0", "A1"], 0: ["A2", "A3"]}[key[2]]
    if key[0] == "wout":
        return ["A0", "A1"] if key[1] < 2 else ["A2", "A3"]
    if key[0] == "xo":
        return ["A2", "A3"] if key[1] == 0 else ["A0", "A1"]
    if key[0] == "up":
        return ["T0", "T1"][key[2]:][:1]
    return ["A0", "A1"] if key[2] == 0 else ["A2", "A3"]


def opens(key):
    if key[0] in ("sv", "dq", "dk", "dv", "xv"):
        return key[1] == 0
    if key[0] == "wout":
        return key[1] % 2 == 0
    if key[0] == "down":
        return key[1] == 0
    return True


def closes(key):
    if key[0] in ("sv", "dq", "dk", "dv", "xv"):
        return key[1] == 1
    if key[0] == "wout":
        return key[1] % 2 == 1
    if key[0] == "down":
        return key[1] == HIDDEN // 512 - 1
    return True


def stage_banks(s):
    return {
        "params": ["X1"], "norm": ["T0", "T1", "X0", "X1"], "ssm_bt": ["A0", "A1"], "ssm_ct": ["A2", "A3"],
        "sb_s": ["X0"], "sb_u": ["X1"], "turn": ["X0", "X1"], "ssm_in": ["A0", "A1"],
        "da_s": ["X0", "X1"], "da_t": ["X1"], "da_o": ["X1"],
    }.get(s[0]) or (
        ["A3"] if s[0] == "sb_p" and s[1] % 2 == 0 else
        ["A2"] if s[0] == "ssm_out" and s[1] % 2 == 0 else
        ["A3"] if s[0] == "da_p" and s[1] % 4 == 0 else
        [["X0", "A0", "A1", "A2"][s[1]]] if s[0] == "xa_s" else
        [["X1", "X0"][s[1] % 2]] if s[0] == "xa_t" else
        [["A0", "A1", "A3", "A2"][s[1]]] if s[0] == "xa_p" else [])


KEYS = [None] * NU
for _k, _i in AT_UNIT.items():
    KEYS[_i] = _k
BANKS = ["A0", "A1", "A2", "A3", "T0", "T1", "X0", "X1"]
USES = {b: [] for b in BANKS}
for _u in range(-1, NU):
    if _u >= 0 and opens(KEYS[_u]):
        for _b in unit_banks(KEYS[_u]):
            USES[_b].append(KEYS[_u] if KEYS[_u][0] != "down" else ("down",))
    for _s in SIDE[_u]:
        for _b in stage_banks(_s):
            USES[_b].append(_s)
OWN_SIGNAL = ("ssm_out", "sb_p", "da_p")
FULLS = {b: [k for k in USES[b] if not (k in AT_UNIT or k == ("down",) or k[0] in OWN_SIGNAL)] for b in BANKS}


class Signal:

    def __init__(self, ctx, nc, name, per_layer, credit=0, step=1):
        self.sem = ctx.enter_context(nc.semaphore(name))
        self.name, self.per_layer, self.credit, self.step, self.made = name, per_layer, credit, step, 0

    def value(self, layer, n):
        return layer * (self.per_layer * self.step) + (n * self.step + self.credit)


class Steps:

    def __init__(self, order, layer=None):
        self.order, self.n, self.last, self.layer = order, 0, None, layer

    def mid(self):
        self.n += 1
        self.last = (self.order, self.n)
        return self.order, 1

    def sig(self, signal, n=None):
        signal.made += 1
        self.last = (signal.sem, signal.value(self.layer, signal.made if n is None else n))
        return signal.sem, 1

    def mark(self, milestones):
        milestones.n += 1
        self.last = (milestones.order, milestones.n)
        return milestones.order, 1

    def at(self, signal, n):
        return signal.sem, signal.value(self.layer, n)

    def mine(self):
        return self.last


def hybrid_trunk(nc, a, out):
    with ExitStack() as ctx:
        def sb(name, shape, dt=F32):
            return ctx.enter_context(nc.sbuf_tensor("s_" + name, shape, dt))

        def sem(name):
            return ctx.enter_context(nc.semaphore(name))

        def signal(name, per_layer, credit=0, step=1):
            s = Signal(ctx, nc, name, per_layer, credit, step)
            signals.append(s)
            return s

        signals = []

        raw = [sb(f"raw{i}", [P, UW]) for i in range(RAW)]
        w_hi = [sb(f"w_hi{i}", [P, UW], F32R) for i in range(HL)]
        w_lo = [sb(f"w_lo{i}", [P, UW], F32R) for i in range(HL)]
        x = sb("x", [P, NT, D])
        memT = sb("memT", [P, KD, T])
        hT_hi, hT_lo = sb("hT_hi", [P, KD, T], F32R), sb("hT_lo", [P, KD, T], F32R)
        bT_hi, bT_lo = sb("bT_hi", [P, 12, T], F32R), sb("bT_lo", [P, 12, T], F32R)
        gates = sb("gates", [P, 16, T])
        qk = sb("qk", [P, KD, T])
        uT = sb("uT", [P, KB, T])
        vN = sb("vN", [P, NT, BW])
        dT = sb("dT", [P, KD, T])
        dv = sb("dv", [P, NT, BW])
        bt = sb("bt", [P, 2, 4, P])
        ct = sb("ct", [P, 2, 4, P])
        pw1 = sb("pw1", [P, 2, STILES, 16])
        pw16 = sb("pw16", [P, 2, STILES, 16])
        rot = sb("rot", [P, 2, 2, 512])
        v_re_im = sb("v_re_im", [P, 2, 512])
        s_re_im = sb("s_re_im", [P, 2, 512])
        tmp = sb("tmp", [P, 2, 512])
        ptmp = sb("ptmp", [P, 512])
        att = sb("att", [P, 2560])
        masks = sb("masks", [P, 3 * P])
        mask_s = masks[:, 0:2 * P]
        mask_n = masks[:, P:3 * P]
        tri = sb("tri", [P, P])
        ones = sb("ones", [P, P])
        ident = sb("ident", [P, P])
        gmask = sb("gmask", [P, P])
        gmaskT = sb("gmaskT", [P, P])
        prm = sb("prm", [P, P])
        ldt = sb("ldt", [P, 2])
        eps = sb("eps", [P, 2])
        col = sb("col", [P, R_END])
        small = sb("small", [P, 24, STILES])
        stat = sb("stat", [P, 64])
        rope = sb("rope", [P, 2, NT, ROT_HALF])
        lam_all = sb("lam_all", [P, 2, DEPTH])
        lam = sb("lam", [P, 2])

        xn = gates[:, 0:8, :].rearrange("p (t k) n -> p t (k n)", t=NT)
        dN = [gates[:, 8 + 4 * i:12 + 4 * i, :].rearrange("p (t k) n -> p t (k n)", t=NT) for i in range(2)]
        bN = gates[:, 0:4, :].rearrange("p (r k) n -> p r (k n)", r=2)
        cN = gates[:, 4:8, :].rearrange("p (r k) n -> p r (k n)", r=2)
        b_raw = s_re_im[:, :, 0:256]
        sg = s_re_im[:, :, :].rearrange("p r (k n) -> p (r k) n", n=T)
        z_b = [att[:, 768 * i:768 * i + 384] for i in range(2)]
        nl_b = [att[:, 768 * i + 384:768 * i + 768] for i in range(2)]
        p_b = [att[:, 1536 + 512 * i:2048 + 512 * i].rearrange("p (c n) -> p c n", c=2) for i in range(2)]
        pT_b = [att[:, 1024 + 256 * i:1280 + 256 * i] for i in range(2)]
        o_b = att[:, 512:1024]
        e_b = [rot[:, h // 2, h % 2, :].rearrange("p (t n) -> p t n", t=NT) for h in range(XA_HEADS)]
        def merged(cb):
            return (bT_hi[:, 0:4, :], bT_lo[:, 0:4, :]) if cb == 0 else (hT_hi[:, 4:8, :], hT_lo[:, 4:8, :])

        def macc(cb, j):
            return rot[:, cb, j, :]

        eT_b = [att[:, 512 * i:512 * i + 512].rearrange("p (m n) -> p m n", m=2) for i in range(XA_HEADS)]
        r_b = [att[:, 512 * i:512 * i + 512] for i in range(2)]
        q_b = [att[:, 1024 + 512 * i:1536 + 512 * i] for i in range(2)]

        bank = {b: ctx.enter_context(nc.psum_tensor("p_" + b, [P, 512], F32)) for b in BANKS}
        full = {b: signal(f"{b}_full", len(FULLS[b])) for b in BANKS}
        free = {b: signal(f"{b}_free", len(USES[b]), credit=1) for b in BANKS}

        raw_landed = [signal(f"raw{i}_landed", NU // RAW, step=16) for i in range(RAW)]
        hi_made = signal("w_hi_made", NU, credit=RAW)
        lo_made = signal("w_lo_made", NU, credit=RAW)
        lo_made_pool = signal("w_lo_made_pool", NU, credit=RAW)
        unit_done = signal("unit_done", NU, credit=HL)
        prm_landed = signal("prm_landed", 9, step=16)
        mat_landed = signal("mat_landed", 6, step=16)
        prm_spread = signal("prm_spread", 1)
        prm_read = signal("prm_read", 1, credit=1)
        norm_r0 = signal("norm_r0", 3)
        norm_ss = signal("norm_ss", 3 * NT * 2)
        diag_ready = signal("diag_ready", 3 * NT)
        norm_hi = signal("norm_hi", 3 * KD)
        dt_ready, lam_dt = signal("dt_ready", 1), signal("lam_dt", 1)
        decay_ready, angle_ready = signal("decay_ready", 1), signal("angle_ready", 1)
        cs_ready, b_ready = signal("cs_ready", 1), signal("b_ready", 1)
        rot_ready = signal("rot_ready", SSM_STEPS)
        rot_used = signal("rot_used", SSM_STEPS, credit=2)
        s_ready = signal("s_ready", SSM_STEPS)
        s_used = signal("s_used", SSM_STEPS, credit=1)
        gelu_hi, gelu_ready = signal("gelu_hi", KB), signal("gelu_ready", KB)
        rope_done = signal("rope_done", 2)
        ln_ready, nl_ready = signal("ln_ready", SB_HEADS), signal("nl_ready", SB_HEADS)
        w_ready, sbp_done = signal("w_ready", SB_HEADS), signal("sbp_done", SB_HEADS)
        sb_hi = signal("sb_hi", SB_HEADS // 2)
        NJ = NT * DA_HEADS
        dmax_ready, dexp_ready = signal("dmax_ready", NJ), signal("dexp_ready", NJ)
        dw_ready, dap_done = signal("dw_ready", NJ), signal("dap_done", NJ)
        oss_ready, o_r0, on_ready = signal("oss_ready", NT), signal("o_r0", NT), signal("on_ready", NT)
        da_hi = signal("da_hi", NT)
        glu_hi, glu_ready = signal("glu_hi", 2), signal("glu_ready", 2)
        gate_ready = signal("gate_ready", 3)
        mg_made, mg_hi, mg_ready = signal("mg_made", 4), signal("mg_hi", 4), signal("mg_ready", 4)
        mem_hi, mem_ready = signal("mem_hi", KD), signal("mem_ready", KD)
        xmax_ready, xw_ready = signal("xmax_ready", XA_HEADS), signal("xw_ready", XA_HEADS)
        xo_hi = signal("xo_hi", XA_HEADS)
        NUP = 2 * (HIDDEN // 512)
        sq_made, hid_hi, hid_ready = signal("sq_made", NUP), signal("hid_hi", NUP), signal("hid_ready", NUP)

        act_order, dve_order, pool_order = sem("act_order"), sem("dve_order"), sem("pool_order")
        x_landed, mem_landed, pos_landed, lam_landed = sem("x_landed"), sem("mem_landed"), sem("pos_landed"), sem("lam_landed")
        sp_held = sem("sp_held")
        nf_landed, stored = sem("nf_landed"), sem("stored")
        consts_made = sem("consts_made")
        pre_pe, pre_act, pre_dve = sem("pre_pe"), sem("pre_act"), sem("pre_dve")
        end_act, end_dve = sem("end_act"), sem("end_dve")

        def full_at(b, stage):
            return full[b], FULLS[b].index(stage) + 1

        def before(b, use):
            return free[b], USES[b].index(use)

        def freed(b, use):
            return free[b], USES[b].index(use) + 1

        def weight_src(u, l):
            mat, kind, kt, cols, k0, c0 = UNITS[u]
            m = a["w_branch"][l, mat[1]] if isinstance(mat, tuple) else a[mat][l]
            return m.rearrange("(k p) n -> p k n", p=P)[:, k0:k0 + kt, c0:c0 + cols]

        def wslot(tile, u):
            return tile[:, :].rearrange("p (k n) -> p k n", k=UNITS[u][2])

        def f32(ap):
            return ap.bitcast(F32)

        gain_row = {"mix": R_MIX, "cross": R_CROSS, "mlp": R_MLP}
        NORMS = ["mix", "cross", "mlp"]
        NORM_BANKS = ["T0", "T1", "X0", "X1"]
        SS, R0, VV, TT, RSTD = (stat[:, 2 * i:2 * i + 2] for i in range(5))
        SS1, SS0V = stat[:, 36:38], stat[:, 38:40]
        dg = [tmp[:, 0, t * P:t * P + P] for t in range(NT)]
        DNB = [stat[:, 10 + 2 * i:12 + 2 * i] for i in range(2)]
        DMX = stat[:, 14:16]
        DRS = [stat[:, 16 + 2 * i:18 + 2 * i] for i in range(2)]
        DRR, DR2 = stat[:, 20:22], stat[:, 22:23]
        XRS = [stat[:, 24 + 2 * i:26 + 2 * i] for i in range(XA_HEADS)]
        XNB = [stat[:, 32 + 2 * i:34 + 2 * i] for i in range(XA_HEADS)]
        OSS, OR0, OVV, OTT, ORSTD = (stat[:, 40 + 4 * i:44 + 4 * i] for i in range(5))
        GSUB = stat[:, 60:61]
        XSCALE, DSCALE = float(P) ** -0.5, float(HD) ** -0.5
        DT, LD, TH, DECAY, KK, THR, THA, SIN, COS, LBR, LBI, DEN, T1, T2, FR, FI = (small[:, i, :] for i in range(16))

        def norm_input(which, half, t):
            if which == "mix":
                return free[f"A{2 * half + t}"], 0
            if which == "cross":
                return freed(f"A{2 * half + t}", ("wout", 2 * half))
            return freed(f"A{2 * (1 - half) + t}", ("xo", half))

        def x_part(t, key):
            cb = {"wout": lambda: key[1] // 2, "xo": lambda: key[1], "down": lambda: key[2]}[key[0]]()
            return x[:, t, 512 * cb:512 * cb + 512]

        block = ctx.enter_context(nc.Block())

        @block.sync
        def _(sp):
            sp.dma_start(x[:, :, :], a["x"][0].rearrange("(t p) d -> p t d", p=P)).then_inc(x_landed, 16)
            sp.dma_start(xn, a["mem"][0].rearrange("(t p) d -> p t d", p=P)).then_inc(mem_landed, 16)
            sp.wait_ge(consts_made, 1)
            with sp.Fori(0, DEPTH) as l:
                st = Steps(None, l)

                def load(dst, src, landed):
                    landed.made += 1
                    sp.dma_start(dst, src).then_inc(landed.sem, 16)

                def load_unit(u):
                    sp.wait_ge(*st.at(hi_made, u - RAW + 1))
                    sp.sem_inc(sp_held, 1)
                    sp.wait_ge(*st.at(lo_made, u - RAW + 1))
                    sp.sem_inc(sp_held, 1)
                    sp.wait_ge(*st.at(lo_made_pool, u - RAW + 1))
                    sp.sem_inc(sp_held, 1)
                    load(wslot(raw[u % RAW], u), weight_src(u, l), raw_landed[u % RAW])

                load_unit(0)
                sp.wait_ge(*st.at(prm_read, 0))
                sp.sem_inc(sp_held, 1)
                for r, name, rows in ((R_MIX, "norm_mix", KD), (R_CROSS, "norm_cross", KD), (R_MEM, "norm_mem", KD),
                                      (R_MLP, "norm_mlp", KD), (R_D, "ssm_d", KB), (R_SUBLN, "diff_subln", 1)):
                    load(prm[r:r + rows, :], a[name][l].rearrange("(r n) -> r n", n=P), prm_landed)
                load(prm[R_LRE:R_LRE + 16, :], a["ssm_lam_re"][l].rearrange("(i g) s -> i (g s)", g=2), prm_landed)
                load(prm[R_LIM:R_LIM + 16, :], a["ssm_lam_im"][l].rearrange("(i g) s -> i (g s)", g=2), prm_landed)
                load(ldt[R_DT:R_DT + 16, :], a["ssm_log_dt"][l].rearrange("(i g) -> i g", g=2), prm_landed)
                for u in range(1, NU):
                    load_unit(u)
                    if u == 4:
                        sp.wait_ge(*st.at(*full_at("X1", ("norm", "mix"))))
                        sp.sem_inc(sp_held, 1)
                        for r, nm in enumerate(("ssm_b_re", "ssm_b_im")):
                            load(b_raw[:, r, :].rearrange("p (i c) -> p i c", c=GC),
                                 a[nm][l].rearrange("(i g) s c -> (g s) i c", g=2), mat_landed)
                        for r, nm in enumerate(("ssm_c_re", "ssm_c_im")):
                            for half in range(2):
                                load(cN[:, r, :].rearrange("p (k h s) -> p k h s", h=2, s=STATES)[:, :, half, :],
                                     a[nm][l].rearrange("(k g) c s -> (g c) k s", g=8), mat_landed)
            sp.wait_ge(unit_done.sem, unit_done.value(DEPTH - 1, AT_UNIT["up", 2, 0]))
            sp.dma_start(uT[:, :, :].rearrange("p k n -> p (k n)"), a["norm_final"].partition_broadcast(P))\
              .then_inc(nf_landed, 16)
            for t in range(NT):
                sp.wait_ge(end_dve, 6 + t)
                sp.dma_start(out[0].rearrange("(t p) d -> p t d", p=P)[:, t, :], xn[:, t, :]).then_inc(stored, 16)
            sp.wait_ge(stored, 16 * NT)

        @block.gpsimd
        def _(pool):
            for s in signals:
                if s.credit:
                    pool.sem_inc(s.sem, s.credit)
            cst = Steps(consts_made)
            nc.gpsimd.memset(prm[:, :], 0.0).then_inc(*cst.mid())
            nc.gpsimd.memset(ident[:, :], 0.0).then_inc(*cst.mid())
            nc.gpsimd.memset(tri[:, :], 1.0).then_inc(*cst.mid())
            nc.gpsimd.memset(ones[:, :], 1.0).then_inc(*cst.mid())
            nc.gpsimd.memset(masks[:, :], BIG).then_inc(*cst.mid())
            nc.gpsimd.memset(gmaskT[:, :], 0.0).then_inc(*cst.mid())
            pool.wait_ge(*cst.mine())
            nc.gpsimd.affine_select(out=ident[:, :], in_=ident[:, :], compare_op=ALU.not_equal, fill=1.0, base=0,
                                          pattern=[[-1, P]], channel_multiplier=1).then_inc(*cst.mid())
            nc.gpsimd.affine_select(out=tri[:, :], in_=tri[:, :], compare_op=ALU.is_ge, fill=0.0, base=0,
                                          pattern=[[-1, P]], channel_multiplier=1).then_inc(*cst.mid())
            nc.gpsimd.affine_select(out=mask_s[:, 0:P], in_=mask_s[:, 0:P], compare_op=ALU.is_ge,
                                          fill=NEG, base=-1, pattern=[[1, P]], channel_multiplier=-1).then_inc(*cst.mid())
            nc.gpsimd.affine_select(out=mask_n[:, P:T], in_=mask_n[:, P:T], compare_op=ALU.is_ge, fill=NEG,
                                          base=0, pattern=[[-1, P]], channel_multiplier=1).then_inc(*cst.mid())
            for half in range(2):
                pool.wait_ge(*cst.mine())
                nc.gpsimd.memset(gmaskT[64 * half:64 * half + 64, :].rearrange(
                    "p (g h c) -> p g h c", h=2, c=GC)[:, :, half, :], 1.0).then_inc(*cst.mid())
            pool.wait_ge(*cst.mine())

            with pool.Fori(0, DEPTH) as l:
                st = Steps(pool_order, l)
                pool.sem_clear(pool_order)

                def tt(o, i0, i1, op=ALU.mult):
                    return nc.gpsimd.tensor_tensor(o, i0, i1, op)

                def prep(u):
                    pool.wait_ge(*st.at(hi_made, u + 1))
                    c = UW - POOL_COLS
                    tt(w_lo[u % HL][:, c:], raw[u % RAW][:, c:], f32(w_hi[u % HL][:, c:]), ALU.subtract).then_inc(*st.sig(lo_made_pool))

                cur = [small[:, 16:18, :], small[:, 18:20, :]]

                def power(k):
                    table, n = (pw1 if k < 4 else pw16), 1 << (k % 4)
                    if k == 0:
                        pool.wait_ge(*st.at(cs_ready, 1))
                        tt(cur[0][:, 0, :], COS, ones[:, 0:STILES]).then_inc(*st.mid())
                        tt(cur[0][:, 1, :], SIN, ones[:, 0:STILES]).then_inc(*st.mid())
                        for tb in (pw1, pw16):
                            nc.gpsimd.memset(tb[:, 0, :, 0:1], 1.0).then_inc(*st.mid())
                            nc.gpsimd.memset(tb[:, 1, :, 0:1], 0.0).then_inc(*st.mid())
                        pool.wait_ge(*st.mine())
                    c = cur[k % 2]
                    cr = c[:, 0, :].unsqueeze(2).broadcast_to([P, STILES, n])
                    ci = c[:, 1, :].unsqueeze(2).broadcast_to([P, STILES, n])
                    er, ei = table[:, 0, :, 0:n], table[:, 1, :, 0:n]

                    def part(i):
                        return ptmp[:, 128 * i:128 * i + STILES * n].rearrange("p (s n) -> p s n", n=n)

                    tt(part(0), er, cr).then_inc(*st.mid())
                    tt(part(1), ei, ci).then_inc(*st.mid())
                    tt(part(2), er, ci).then_inc(*st.mid())
                    tt(part(3), ei, cr).then_inc(*st.mid())
                    sq = [small[:, 20 + i, :] for i in range(3)]
                    if k < 7:
                        tt(sq[0], c[:, 0, :], c[:, 0, :]).then_inc(*st.mid())
                        tt(sq[1], c[:, 1, :], c[:, 1, :]).then_inc(*st.mid())
                        tt(sq[2], c[:, 0, :], c[:, 1, :]).then_inc(*st.mid())
                    pool.wait_ge(*st.mine())
                    tt(table[:, 0, :, n:2 * n], part(0), part(1), ALU.subtract).then_inc(*st.mid())
                    tt(table[:, 1, :, n:2 * n], part(2), part(3), ALU.add).then_inc(*st.mid())
                    if k < 7:
                        nxt = cur[(k + 1) % 2]
                        tt(nxt[:, 0, :], sq[0], sq[1], ALU.subtract).then_inc(*st.mid())
                        tt(nxt[:, 1, :], sq[2], sq[2], ALU.add).then_inc(*st.mid())
                    pool.wait_ge(*st.mine())

                def rotations(i):
                    pool.wait_ge(*st.at(rot_used, i - 1))
                    ar, ai = (pw16[:, r, 2 * i:2 * i + 2, :].unsqueeze(3).broadcast_to([P, 2, 16, 16]) for r in (0, 1))
                    br, bi = (pw1[:, r, 2 * i:2 * i + 2, :].unsqueeze(2).broadcast_to([P, 2, 16, 16]) for r in (0, 1))
                    o = [rot[:, i % 2, r, :].rearrange("p (s a b) -> p s a b", a=16, b=16) for r in (0, 1)]
                    pt = ptmp[:, :].rearrange("p (s a b) -> p s a b", a=16, b=16)
                    tt(o[0], ar, br).then_inc(*st.mid())
                    tt(pt, ai, bi).then_inc(*st.mid())
                    pool.wait_ge(*st.mine())
                    tt(o[0], o[0], pt, ALU.subtract).then_inc(*st.mid())
                    tt(o[1], ar, bi).then_inc(*st.mid())
                    pool.wait_ge(*st.mine())
                    tt(pt, ai, br).then_inc(*st.mid())
                    pool.wait_ge(*st.mine())
                    tt(o[1], o[1], pt, ALU.add).then_inc(*st.sig(rot_ready))

                def rotate(w):
                    key = ("dq", "dk")[w]
                    pool.wait_ge(*st.at(*freed("T0", (key, 0))))
                    pool.wait_ge(*st.at(*freed("T1", (key, 0))))
                    v = dN[w].rearrange("p t (c d) -> p t c d", d=HD)
                    t1, t2 = v[:, :, :, 0:ROT_HALF], v[:, :, :, ROT_HALF:ROT]
                    cs = [rope[:, i, :, :].unsqueeze(2).broadcast_to([P, NT, 8, ROT_HALF]) for i in (0, 1)]
                    h = [ptmp[:, 128 * i:128 * i + 128].rearrange("p (t c d) -> p t c d", t=NT, c=8) for i in (0, 1)]
                    tt(h[0], t2, cs[1]).then_inc(*st.mid())
                    tt(h[1], t1, cs[1]).then_inc(*st.mid())
                    pool.wait_ge(*st.mine())
                    tt(t1, t1, cs[0]).then_inc(*st.mid())
                    tt(t2, t2, cs[0]).then_inc(*st.mid())
                    pool.wait_ge(*st.mine())
                    tt(t1, t1, h[0], ALU.subtract).then_inc(*st.mid())
                    tt(t2, t2, h[1], ALU.add).then_inc(*st.sig(rope_done))

                for u in range(-1, NU):
                    if u < 0:
                        prep(0)
                        prep(1)
                    elif u + HL < NU:
                        prep(u + HL)
                    for s in SIDE[u]:
                        pool.wait_ge(*st.mine())
                        if s[0] == "ssm_pow":
                            power(s[1])
                            if s[1] == 7:
                                rotations(0)
                        elif s[0] == "ssm_in" and s[1] + 1 < SSM_STEPS:
                            rotations(s[1] + 1)
                        elif s[0] == "rope":
                            rotate(s[1])
                pool.wait_ge(*st.mine())

        @block.scalar
        def _(act):
            def fn(o, i, f=ACT.Copy, **kw):
                return nc.scalar.activation(o, i, f, **kw)

            ast = Steps(pre_act)
            act.dma_start(att[:, 0:512], a["diff_lambda"].rearrange("l k n -> (l k n)").partition_broadcast(P))\
               .then_inc(lam_landed, 16)
            act.dma_start(stat[:, 62:64].bitcast(I32), a["positions"][0].rearrange("(t p) -> p t", p=P),
                          allow_slow_non_contiguous=True).then_inc(pos_landed, 16)
            act.preload_act_table_set("natural_log_exp_and_others")
            act.wait_ge(pre_dve, 1)
            act.wait_ge(mem_landed, 16)
            for t in range(NT):
                fn(memT[:, 4 * t:4 * t + 4, :].rearrange("p k n -> p (k n)"), xn[:, t, :], ACT.Square,
                        accum_out=SS[:, t:t + 1]).then_inc(*ast.mid())
                act.wait_ge(*ast.mine())
            fn(R0, SS, ACT.Ln, scale=1.0 / D, bias=eps[:, 0:1]).then_inc(*ast.mid())
            act.wait_ge(*ast.mine())
            fn(R0, R0, ACT.Exp, scale=-0.5).then_inc(*ast.mid())
            act.wait_ge(*ast.mine())
            act.wait_ge(pre_dve, 2)
            fn(stat[:, 28:32], stat[:, 24:28], ACT.Exp).then_inc(*ast.mid())
            act.wait_ge(*ast.mine())
            act.wait_ge(pre_dve, 4)
            rp = [rope[:, i, :, :].rearrange("p t j -> p (t j)") for i in (0, 1)]
            fn(rp[0], small[:, 5, :], ACT.Abs).then_inc(*ast.mid())
            act.wait_ge(*ast.mine())
            fn(rp[1], small[:, 5, :], ACT.Sin).then_inc(*ast.mid())
            act.wait_ge(*ast.mine())
            fn(rp[0], rp[0], ACT.Sin, scale=-1.0, bias=eps[:, 1:2]).then_inc(*ast.mid())
            act.wait_ge(*ast.mine())

            act.wait_ge(x_landed, 16)
            act.wait_ge(pre_dve, 11)

            with act.Fori(0, DEPTH) as l:
                st = Steps(act_order, l)
                act.sem_clear(act_order)

                def prep(u):
                    act.wait_ge(*st.at(raw_landed[u % RAW], u // RAW + 1))
                    act.wait_ge(*st.at(unit_done, u - HL + 1))
                    fn(w_hi[u % HL][:, :], raw[u % RAW][:, :]).then_inc(*st.sig(hi_made))

                def stats(which, half):
                    for t in range(NT):
                        act.wait_ge(*st.at(*norm_input(which, half, t)))
                        c = slice(512 * half, 512 * half + 512)
                        fn(xn[:, t, c], x[:, t, c], ACT.Square, accum_out=(SS1 if half else SS)[:, t:t + 1])\
                            .then_inc(*st.sig(norm_ss))
                    if half == 0:
                        act.preload_act_table_set("natural_log_exp_and_others")
                    act.wait_ge(*st.mine())
                    if half == 0:
                        fn(SS0V, SS, ACT.Identity, scale=1.0 / D, bias=eps[:, 0:1]).then_inc(*st.mid())
                    else:
                        for t in range(NT):
                            fn(R0[:, t:t + 1], SS1[:, t:t + 1], ACT.Ln, scale=1.0 / D, bias=SS0V[:, t:t + 1])\
                                .then_inc(*st.mid())
                        act.wait_ge(*st.mine())
                        fn(R0, R0, ACT.Exp, scale=-0.5).then_inc(*st.sig(norm_r0))

                def norm(which):
                    if which == "mix":
                        act.wait_ge(*st.at(*freed("X1", ("params",))))
                    g = gain_row[which]
                    for j, b in enumerate(NORM_BANKS):
                        act.wait_ge(*st.at(*full_at(b, ("norm", which))))
                        for k in (2 * j, 2 * j + 1):
                            fn(hT_hi[:, k, :], bank[b][:, (k % 2) * T:(k % 2) * T + T], ACT.Identity,
                               scale=col[:, g + k:g + k + 1]).then_inc(*st.sig(norm_hi))

                def ssm_prep():
                    fn(DT, col[:, R_DT:R_DT + 16], ACT.Exp).then_inc(*st.sig(dt_ready))
                    act.wait_ge(*st.at(lam_dt, 1))
                    fn(DECAY, LD, ACT.Exp).then_inc(*st.sig(decay_ready))
                    act.wait_ge(*st.at(angle_ready, 1))
                    fn(THA, THR, ACT.Abs).then_inc(*st.mid())
                    fn(SIN, THR, ACT.Sin).then_inc(*st.mid())
                    act.wait_ge(*st.mine())
                    fn(COS, THA, ACT.Sin, scale=-1.0, bias=eps[:, 1:2]).then_inc(*st.sig(cs_ready))
                    act.preload_act_table_set("natural_log_exp_and_others")

                def evac(u):
                    key = KEYS[u]
                    if not closes(key):
                        return
                    b = unit_banks(key)
                    kind, use = key[0], (key[0], 0)

                    def take(o, bk, use, f=ACT.Copy, **kw):
                        act.wait_ge(*st.at(unit_done, u + 1))
                        fn(o, bank[bk][:, :], f, **kw).then_inc(*st.sig(*freed(bk, use)))

                    def flat(o):
                        return o.rearrange("p k n -> p (k n)")

                    if kind == "sq":
                        take(flat(qk[:, 2 * key[1]:2 * key[1] + 2, :]), b[0], key, scale=DSCALE)
                    elif kind == "sv" or kind == "xv":
                        take(vN[:, 0, :], "T0", use)
                    elif kind in ("dq", "dk"):
                        take(dN[kind == "dk"][:, 0, :], "T0", use)
                    elif kind == "dv":
                        take(dv[:, 0, :], "T0", use)
                    elif isinstance(kind, tuple):
                        n, i = kind[1], key[1]
                        dst = qk if n == 0 else gates
                        k0 = 2 * i + (8 if n == 2 else 0)
                        take(flat(dst[:, k0:k0 + 2, :]), b[0], key)
                    elif key == ("glu", 1):
                        for j, bk in enumerate(b):
                            take(flat(sg[:, 2 * j:2 * j + 2, :]), bk, key, ACT.Sigmoid)
                    elif key == ("glu", 0):
                        fn(flat(gates[:, 0:8, :]), flat(gates[:, 0:8, :]), ACT.Sigmoid).then_inc(*st.sig(gate_ready))
                        for j, bk in enumerate(b):
                            act.wait_ge(*st.at(*freed(bk, key)))
                            fn(flat(hT_hi[:, 2 * j:2 * j + 2, :]), v_re_im[:, j, :]).then_inc(*st.sig(glu_hi))
                    elif kind == "branch":
                        cb, n = key[1:]
                        if cb == 0 and n == 1:
                            fn(flat(gates[:, 8:16, :]), flat(gates[:, 8:16, :]), ACT.Sigmoid).then_inc(*st.sig(gate_ready))
                        if cb == 0 and n == 2:
                            fn(flat(qk[:, :, :]), flat(qk[:, :, :]), ACT.Sigmoid).then_inc(*st.sig(gate_ready))
                        if n == 0:
                            for j in range(2):
                                act.wait_ge(*st.at(mg_made, 2 * cb + j + 1))
                                fn(flat(merged(cb)[0][:, 2 * j:2 * j + 2, :]), macc(cb, j)).then_inc(*st.sig(mg_hi))
                    elif kind == "xq":
                        take(flat(qk[:, 2 * key[1]:2 * key[1] + 2, :]), b[0], key)
                    elif kind == "up":
                        g, i = key[1:]
                        if g:
                            act.wait_ge(*st.at(sq_made, 2 * g + i - 1))
                        take(r_b[i], b[0], key, ACT.Relu)
                        act.wait_ge(*st.at(sq_made, 2 * g + i + 1))
                        if g >= 2:
                            act.wait_ge(*st.at(unit_done, AT_UNIT["down", g - 2, 1] + 1))
                        k0 = 4 * (g % 2) + 2 * i
                        fn(flat(bT_hi[:, k0:k0 + 2, :]), q_b[i]).then_inc(*st.sig(hid_hi))

                def stage(s):
                    kind = s[0]
                    if kind == "stats":
                        stats(*s[1:])
                    elif kind == "norm":
                        norm(s[1])
                    elif kind == "ssm_prep":
                        ssm_prep()
                    elif kind == "turn":
                        act.wait_ge(*st.at(*full_at("X0", s)))
                        fn(dT[:, 4 * s[1]:4 * s[1] + 2, :].rearrange("p k n -> p (k n)"), bank["X0"][:, :]).then_inc(*st.sig(*freed("X0", s)))
                    elif kind == "sb_u":
                        z = z_b[s[1] % 2]
                        act.wait_ge(*st.at(*freed("X1", s)))
                        fn(z, z, ACT.Exp).then_inc(*st.sig(w_ready))
                    elif kind == "sb_p" and s[1] % 2:
                        act.wait_ge(*st.at(sbp_done, s[1] + 1))
                        fn(bT_hi[:, 4 + s[1] // 2, :], bank["A3"][:, 0:T]).then_inc(*st.sig(sb_hi))
                    elif kind == "da_t":
                        j = s[1]
                        nk = P * (j // DA_HEADS + 1)
                        act.wait_ge(*st.at(*full_at("X1", s)))
                        if j >= 2:
                            act.wait_ge(*st.at(dap_done, j - 1))
                        fn(pT_b[j % 2][:, 0:nk], bank["X1"][:, 0:nk]).then_inc(*st.sig(*freed("X1", s)))
                    elif kind == "da_n":
                        qt = s[1]
                        act.wait_ge(*st.at(oss_ready, qt + 1))
                        fn(OR0, OSS, ACT.Ln, scale=1.0 / P, bias=eps[:, 0:1]).then_inc(*st.mid())
                        act.wait_ge(*st.mine())
                        fn(OR0, OR0, ACT.Exp, scale=-0.5).then_inc(*st.sig(o_r0))
                    elif kind == "da_o":
                        qt = s[1]
                        act.wait_ge(*st.at(*full_at("X1", s)))
                        fn(bT_hi[:, 8:12, qt * P:qt * P + P], bank["X1"][:, :].rearrange("p (h n) -> p h n", n=P),
                                  ACT.Identity, scale=GSUB).then_inc(*st.sig(da_hi))
                    elif kind == "gelu":
                        act.wait_ge(*st.at(*freed("A2", ("ssm_out", SSM_STEPS - 2))))
                        gl = v_re_im[:, :, :].rearrange("p r (k n) -> p (r k) n", n=T)
                        for k in range(KB):
                            fn(gl[:, k, :], uT[:, k, :], ACT.Gelu_apprx_tanh).then_inc(*st.mid())
                        act.wait_ge(*st.mine())
                        for k in range(KB):
                            fn(bT_hi[:, k, :], gl[:, k, :]).then_inc(*st.sig(gelu_hi))
                        act.preload_act_table_set("natural_log_exp_and_others")
                    elif kind == "memg":
                        act.wait_ge(*st.at(unit_done, AT_UNIT["branch", 1, 0] + 1))
                        for k in range(KD):
                            fn(bT_hi[:, 4 + k, :], memT[:, k, :], ACT.Identity,
                                      scale=col[:, R_MEM + k:R_MEM + k + 1]).then_inc(*st.sig(mem_hi))
                    elif kind == "xa_s":
                        h = s[1]
                        b = stage_banks(s)[0]
                        act.wait_ge(*st.at(xmax_ready, h + 1))
                        for qt in range(NT):
                            ins = fn(e_b[h][:, qt, :], bank[b][:, qt * T:qt * T + T], ACT.Exp, scale=XSCALE,
                                     bias=XNB[h][:, qt:qt + 1], accum_out=XRS[h][:, qt:qt + 1])
                            ins.then_inc(*st.sig(*freed(b, s))) if qt else ins.then_inc(*st.mid())
                    elif kind == "xa_t":
                        h = s[1]
                        b = stage_banks(s)[0]
                        act.wait_ge(*st.at(*full_at(b, s)))
                        fn(eT_b[h].rearrange("p m n -> p (m n)"), bank[b][:, :]).then_inc(*st.sig(*freed(b, s)))
                    elif kind == "xa_p":
                        h = s[1]
                        b = stage_banks(s)[0]
                        act.wait_ge(*st.at(*full_at(b, s)))
                        fn(bT_hi[:, h, :], bank[b][:, 0:T]).then_inc(*st.sig(xo_hi))

                def later(s):
                    kind = s[0]
                    if kind == "sb_s":
                        z, nl = z_b[s[1] % 2], nl_b[s[1] % 2]
                        act.wait_ge(*st.at(*freed("X0", s)))
                        fn(nl, z, ACT.Abs).then_inc(*st.mid())
                        act.wait_ge(*st.mine())
                        fn(nl, nl, ACT.Exp, scale=-1.0).then_inc(*st.mid())
                        act.wait_ge(*st.mine())
                        fn(nl, nl, ACT.Ln, bias=1.0).then_inc(*st.sig(ln_ready))
                    elif kind == "da_s":
                        j = s[1]
                        nk = P * (j // DA_HEADS + 1)
                        act.wait_ge(*st.at(dmax_ready, j + 1))
                        for c in range(2):
                            ins = fn(p_b[j % 2][:, c, 0:nk], p_b[j % 2][:, c, 0:nk], ACT.Exp, scale=DSCALE,
                                     bias=DNB[j % 2][:, c:c + 1], accum_out=DRS[j % 2][:, c:c + 1])
                            ins.then_inc(*st.sig(dexp_ready)) if c else ins.then_inc(*st.mid())

                prep(0)
                prep(1)
                for u in range(-1, NU):
                    preps = 0 <= u < NU - HL
                    if preps and u not in STAGES_FIRST:
                        prep(u + HL)
                    if u >= 0:
                        evac(u)
                    for s in SIDE[u]:
                        act.wait_ge(*st.mine())
                        stage(s)
                    if preps and u in STAGES_FIRST:
                        prep(u + HL)
                    for s in SIDE[u]:
                        act.wait_ge(*st.mine())
                        later(s)
                act.wait_ge(*st.mine())
            for b in ("A0", "A1", "A2", "A3"):
                act.wait_ge(free[b].sem, free[b].value(DEPTH, 0))
            for t in range(NT):
                fn(xn[:, t, :], x[:, t, :], ACT.Square, accum_out=SS[:, t:t + 1]).then_inc(end_act, 1)
            act.wait_ge(end_act, 2)
            act.preload_act_table_set("natural_log_exp_and_others")
            fn(R0, SS, ACT.Ln, scale=1.0 / D, bias=eps[:, 0:1]).then_inc(end_act, 1)
            act.wait_ge(end_act, 3)
            fn(R0, R0, ACT.Exp, scale=-0.5).then_inc(end_act, 1)

        @block.vector
        def _(dve):
            V = nc.vector

            def newton(c, r0, ss, n, v, t, r):
                V.tensor_scalar(v, ss, 1.0 / n, RMS_EPS, ALU.mult, ALU.add).then_inc(*c.mid())
                V.tensor_tensor(t, r0, r0, ALU.mult).then_inc(*c.mid())
                dve.wait_ge(*c.mine())
                V.tensor_tensor(t, t, v, ALU.mult).then_inc(*c.mid())
                dve.wait_ge(*c.mine())
                V.tensor_scalar(t, t, -0.5, 1.5, ALU.mult, ALU.add).then_inc(*c.mid())
                dve.wait_ge(*c.mine())
                V.tensor_tensor(r, r0, t, ALU.mult).then_inc(*c.mid())
                dve.wait_ge(*c.mine())

            def reduce_angle(c, th, k, o):
                V.tensor_scalar(k, th, 1.0 / TWO_PI, ROUND, ALU.mult, ALU.add).then_inc(*c.mid())
                dve.wait_ge(*c.mine())
                V.tensor_scalar(k, k, ROUND, None, ALU.subtract).then_inc(*c.mid())
                dve.wait_ge(*c.mine())
                V.scalar_tensor_tensor(out=o, in0=k, scalar=-PI_HI, in1=th, op0=ALU.mult, op1=ALU.add)\
                 .then_inc(*c.mid())
                dve.wait_ge(*c.mine())
                V.scalar_tensor_tensor(out=o, in0=k, scalar=-PI_MID, in1=o, op0=ALU.mult, op1=ALU.add)\
                 .then_inc(*c.mid())
                dve.wait_ge(*c.mine())
                V.scalar_tensor_tensor(out=o, in0=k, scalar=-PI_LO, in1=o, op0=ALU.mult, op1=ALU.add)\
                 .then_inc(*c.mid())
                dve.wait_ge(*c.mine())

            pst, mst = Steps(dve_order), Steps(pre_dve)

            V.memset(eps[:, 0:1], RMS_EPS).then_inc(*pst.mid())
            V.memset(eps[:, 1:2], math.pi / 2).then_inc(*pst.mid())
            V.memset(small[:, :, :], 0.0).then_inc(*pst.mark(mst))
            dve.wait_ge(*pst.mine())
            dve.wait_ge(lam_landed, 16)
            lv = att[:, 0:512].rearrange("p (m b n) -> p m b n", b=2, n=HD)
            pr = att[:, 512:768].rearrange("p (m n) -> p m n", n=HD)
            V.tensor_tensor(pr, lv[:, :, 0, :], lv[:, :, 1, :], ALU.mult).then_inc(*pst.mid())
            dve.wait_ge(*pst.mine())
            V.tensor_reduce(stat[:, 24:28], pr, AX.X, ALU.add).then_inc(*pst.mark(mst))
            dve.wait_ge(pos_landed, 16)
            V.tensor_copy(stat[:, 10:12], stat[:, 62:64].bitcast(I32)).then_inc(*pst.mid())
            dve.wait_ge(*pst.mine())
            inv = (np.float32(ROPE_THETA) ** (-np.arange(0, ROT, 2, dtype=np.float32) / np.float32(ROT))).astype(np.float32)
            ang = small[:, 4, :].rearrange("p (t j) -> p t j", t=NT)
            for j in range(ROT_HALF):
                V.tensor_scalar(ang[:, :, j], stat[:, 10:12], float(inv[j]), None, ALU.mult).then_inc(*pst.mid())
            dve.wait_ge(*pst.mine())
            V.tensor_copy(small[:, 3, :], small[:, 4, :]).then_inc(*pst.mark(mst))
            dve.wait_ge(*pst.mine())
            reduce_angle(pst, small[:, 3, :], small[:, 4, :], small[:, 5, :])
            V.tensor_scalar(small[:, 5, :], small[:, 5, :], PI_SAFE, -PI_SAFE, ALU.min, ALU.max).then_inc(*pst.mark(mst))
            dve.wait_ge(pre_act, 5)
            for i in range(DEPTH):
                init = 0.8 - 0.6 * math.exp(-0.3 * i)
                e0, e1 = stat[:, 28 + 2 * i:29 + 2 * i], stat[:, 29 + 2 * i:30 + 2 * i]
                V.tensor_tensor(lam_all[:, 0, i:i + 1], e1, e0, ALU.subtract).then_inc(*pst.mid())
                dve.wait_ge(*pst.mine())
                V.tensor_scalar(lam_all[:, 0, i:i + 1], lam_all[:, 0, i:i + 1], init, None, ALU.subtract).then_inc(*pst.mid())
                V.memset(lam_all[:, 1, i:i + 1], 1.0 - init).then_inc(*pst.mid())
            dve.wait_ge(consts_made, 12)
            newton(pst, R0, SS, D, VV, TT, RSTD)
            for t in range(NT):
                V.tensor_scalar(dg[t], ident[:, :], RSTD[:, t:t + 1], None, ALU.mult).then_inc(*pst.mark(mst))
            dve.wait_ge(pre_pe, 1)
            V.tensor_copy(gmask[:, :], bank["A0"][:, 0:P]).then_inc(*pst.mark(mst))
            for j, b in enumerate(NORM_BANKS):
                dve.wait_ge(pre_pe, 2 + j)
                V.tensor_copy(memT[:, 2 * j:2 * j + 2, :].rearrange("p k n -> p (k n)"), bank[b][:, :]).then_inc(*pst.mark(mst))
            dve.wait_ge(*pst.mine())
            dve.wait_ge(x_landed, 16)

            with dve.Fori(0, DEPTH) as l:
                st = Steps(dve_order, l)
                dve.sem_clear(dve_order)

                def tt(o, i0, i1, op=ALU.mult):
                    return V.tensor_tensor(o, i0, i1, op)

                def flat(o):
                    return o.rearrange("p k n -> p (k n)")

                def prep(u):
                    dve.wait_ge(*st.at(hi_made, u + 1))
                    c = UW - POOL_COLS
                    tt(w_lo[u % HL][:, 0:c], raw[u % RAW][:, 0:c], f32(w_hi[u % HL][:, 0:c]), ALU.subtract).then_inc(*st.sig(lo_made))

                def params():
                    dve.wait_ge(*st.at(prm_landed, 9))
                    V.tensor_copy(prm[R_DT:R_DT + 16, :].rearrange("p (g s) -> p g s", g=2),
                                         ldt[R_DT:R_DT + 16, :].unsqueeze(2).broadcast_to([16, 2, STATES])).then_inc(*st.sig(prm_spread))
                    dve.wait_ge(*st.at(*full_at("X1", ("params",))))
                    V.tensor_copy(col[:, :], bank["X1"][:, 0:R_END]).then_inc(*st.sig(*freed("X1", ("params",))))
                    dve.wait_ge(*st.mine())
                    V.tensor_copy(lam[:, :], lam_all[:, :, bass.ds(l, 1)].rearrange("p a b -> p (a b)")).then_inc(*st.mid())
                    dve.wait_ge(*st.mine())
                    tt(GSUB, col[:, R_SUBLN:R_SUBLN + 1], lam[:, 1:2]).then_inc(*st.sig(prm_read))

                def stats(which):
                    n = NORMS.index(which)
                    dve.wait_ge(*st.at(norm_ss, 2 * NT * (n + 1)))
                    V.scalar_tensor_tensor(out=VV, in0=SS1, scalar=1.0 / D, in1=SS0V, op0=ALU.mult, op1=ALU.add)\
                     .then_inc(*st.mid())
                    dve.wait_ge(*st.mine())
                    dve.wait_ge(*st.at(norm_r0, n + 1))
                    for t in range(NT):
                        V.scalar_tensor_tensor(out=TT[:, t:t + 1], in0=R0[:, t:t + 1], scalar=R0[:, t:t + 1],
                                               in1=VV[:, t:t + 1], op0=ALU.mult, op1=ALU.mult).then_inc(*st.mid())
                    dve.wait_ge(*st.mine())
                    V.tensor_scalar(TT, TT, -0.5, 1.5, ALU.mult, ALU.add).then_inc(*st.mid())
                    dve.wait_ge(*st.mine())
                    for t in range(NT):
                        V.tensor_scalar(dg[t], ident[:, :], R0[:, t:t + 1], TT[:, t:t + 1], ALU.mult, ALU.mult)\
                         .then_inc(*st.sig(diag_ready))

                def norm(which):
                    n = NORMS.index(which)
                    g = gain_row[which]
                    for j, b in enumerate(NORM_BANKS):
                        dve.wait_ge(*st.at(norm_hi, KD * n + 2 * j + 2))
                        for k in (2 * j, 2 * j + 1):
                            ins = V.scalar_tensor_tensor(
                                out=hT_lo[:, k, :], in0=bank[b][:, (k % 2) * T:(k % 2) * T + T],
                                scalar=col[:, g + k:g + k + 1], in1=f32(hT_hi[:, k, :]), op0=ALU.mult, op1=ALU.subtract)
                            ins.then_inc(*st.sig(*freed(b, ("norm", which)))) if k % 2 else ins.then_inc(*st.mid())

                def ssm_prep():
                    lre, lim = col[:, R_LRE:R_LRE + 16], col[:, R_LIM:R_LIM + 16]
                    dve.wait_ge(*st.at(dt_ready, 1))
                    tt(LD, lre, DT).then_inc(*st.mid())
                    tt(TH, lim, DT).then_inc(*st.sig(lam_dt))
                    dve.wait_ge(*st.mine())
                    reduce_angle(st, TH, KK, THR)
                    V.tensor_scalar(THR, THR, PI_SAFE, -PI_SAFE, ALU.min, ALU.max).then_inc(*st.sig(angle_ready))
                    dve.wait_ge(*st.at(cs_ready, 1))
                    tt(LBR, DECAY, COS).then_inc(*st.mid())
                    tt(LBI, DECAY, SIN).then_inc(*st.mid())
                    tt(T1, lre, lre).then_inc(*st.mid())
                    tt(T2, lim, lim).then_inc(*st.mid())
                    dve.wait_ge(*st.mine())
                    V.tensor_scalar(LBR, LBR, -1.0, None, ALU.add).then_inc(*st.mid())
                    tt(DEN, T1, T2, ALU.add).then_inc(*st.mid())
                    dve.wait_ge(*st.mine())
                    V.reciprocal(DEN, DEN).then_inc(*st.mid())
                    tt(T1, LBR, lre).then_inc(*st.mid())
                    tt(T2, LBI, lim).then_inc(*st.mid())
                    dve.wait_ge(*st.mine())
                    tt(FR, T1, T2, ALU.add).then_inc(*st.mid())
                    dve.wait_ge(*st.mine())
                    tt(T1, LBI, lre).then_inc(*st.mid())
                    tt(T2, LBR, lim).then_inc(*st.mid())
                    dve.wait_ge(*st.mine())
                    tt(FI, T1, T2, ALU.subtract).then_inc(*st.mid())
                    dve.wait_ge(*st.mine())
                    tt(FR, FR, DEN).then_inc(*st.mid())
                    tt(FI, FI, DEN).then_inc(*st.mid())

                def ssm_bt():
                    dve.wait_ge(*st.at(mat_landed, 6))
                    dve.wait_ge(*st.mine())

                    def bb(i):
                        return b_raw[:, i, :].rearrange("p (i c) -> p i c", c=GC)

                    def prod(i):
                        return tmp[:, i, 0:256].rearrange("p (i c) -> p i c", c=GC)

                    def dup(t3):
                        return t3.unsqueeze(2).broadcast_to([P, STILES, 2, GC])

                    fr, fi = (f.unsqueeze(2).broadcast_to([P, STILES, GC]) for f in (FR, FI))
                    for r, (f0, f1, op) in enumerate(((fr, fi, ALU.subtract), (fi, fr, ALU.add))):
                        tt(prod(0), bb(0), f0).then_inc(*st.mid())
                        tt(prod(1), bb(1), f1).then_inc(*st.mid())
                        dve.wait_ge(*st.mine())
                        ins = tt(bN[:, r, :].rearrange("p (i h c) -> p i h c", h=2, c=GC), dup(prod(0)), dup(prod(1)), op)
                        ins.then_inc(*st.sig(b_ready)) if r else ins.then_inc(*st.mid())
                        dve.wait_ge(*st.mine())
                    for r, b in enumerate(("A0", "A1")):
                        dve.wait_ge(*st.at(*full_at(b, ("ssm_bt",))))
                        tt(bt[:, r, :, :], bank[b][:, :].rearrange("p (k n) -> p k n", n=P),
                                  gmask[:, :].unsqueeze(1).broadcast_to([P, 4, P])).then_inc(*st.sig(*freed(b, ("ssm_bt",))))

                def ssm_ct():
                    for r, b in enumerate(("A2", "A3")):
                        dve.wait_ge(*st.at(*full_at(b, ("ssm_ct",))))
                        for k in range(4):
                            ins = V.scalar_tensor_tensor(out=ct[:, r, k, :], in0=bank[b][:, k * P:k * P + P],
                                                         scalar=(-1.0 if r else 1.0), in1=gmaskT[:, :],
                                                         op0=ALU.mult, op1=ALU.mult)
                            ins.then_inc(*st.sig(*freed(b, ("ssm_ct",)))) if k == 3 else ins.then_inc(*st.mid())

                def ssm_in(i):
                    s = ("ssm_in", i)
                    cs, sn = rot[:, i % 2, 0, :], rot[:, i % 2, 1, :]
                    dve.wait_ge(*st.at(rot_ready, i + 1))
                    dve.wait_ge(*st.mine())
                    for j, b in enumerate(("A0", "A1")):
                        c = slice(j * T, j * T + T)
                        io = bank[b][:, :].rearrange("p (r n) -> p r n", r=2)
                        dve.wait_ge(*st.at(*full_at(b, s)))
                        tt(v_re_im[:, :, c], io, cs[:, c].unsqueeze(1).broadcast_to([P, 2, T])).then_inc(*st.mid())
                        tt(tmp[:, :, c], io, sn[:, c].unsqueeze(1).broadcast_to([P, 2, T])).then_inc(*st.sig(*freed(b, s)))
                    dve.wait_ge(*st.mine())
                    tt(v_re_im[:, 0, :], v_re_im[:, 0, :], tmp[:, 1, :], ALU.add).then_inc(*st.mid())
                    tt(v_re_im[:, 1, :], v_re_im[:, 1, :], tmp[:, 0, :], ALU.subtract).then_inc(*st.mid())
                    dve.wait_ge(*st.mine())
                    for r in range(2):
                        for j in range(2):
                            vt = v_re_im[:, r, j * T:j * T + T]
                            V.tensor_tensor_scan(vt, DECAY[:, 2 * i + j:2 * i + j + 1].broadcast_to([P, T]), vt,
                                                        0.0, ALU.mult, ALU.add).then_inc(*st.mid())

                def ssm_rot(i):
                    cs, sn = rot[:, i % 2, 0, :], rot[:, i % 2, 1, :]
                    dve.wait_ge(*st.at(s_used, i))
                    dve.wait_ge(*st.mine())
                    tt(s_re_im[:, 0, :], v_re_im[:, 0, :], cs).then_inc(*st.mid())
                    tt(tmp[:, 0, :], v_re_im[:, 1, :], sn).then_inc(*st.mid())
                    tt(s_re_im[:, 1, :], v_re_im[:, 0, :], sn).then_inc(*st.mid())
                    tt(tmp[:, 1, :], v_re_im[:, 1, :], cs).then_inc(*st.sig(rot_used))
                    dve.wait_ge(*st.mine())
                    tt(s_re_im[:, 0, :], s_re_im[:, 0, :], tmp[:, 0, :], ALU.subtract).then_inc(*st.mid())
                    tt(s_re_im[:, 1, :], s_re_im[:, 1, :], tmp[:, 1, :], ALU.add).then_inc(*st.sig(s_ready))

                def residual(key, banks):
                    dve.wait_ge(*st.at(unit_done, AT_UNIT[key] + 1))
                    for t, b in enumerate(banks):
                        use = ("down",) if key[0] == "down" else ("wout", key[1] - 1) if key[0] == "wout" else key
                        tt(x_part(t, key), x_part(t, key), bank[b][:, :], ALU.add).then_inc(*st.sig(*freed(b, use)))

                def evac(u):
                    key = KEYS[u]
                    if not closes(key):
                        return
                    b = unit_banks(key)
                    kind, use = key[0], (key[0], 0)

                    def take(o, bk, use):
                        dve.wait_ge(*st.at(unit_done, u + 1))
                        V.tensor_copy(o, bank[bk][:, :]).then_inc(*st.sig(*freed(bk, use)))

                    if kind == "u":
                        take(flat(uT[:, 2 * key[1]:2 * key[1] + 2, :]), b[0], key)
                    elif kind in ("sk", "xk"):
                        take(flat(qk[:, 4 + 2 * key[1]:6 + 2 * key[1], :]), b[0], key)
                    elif kind in ("sv", "xv"):
                        take(vN[:, 1, :], "T1", use)
                    elif kind in ("dq", "dk"):
                        take(dN[kind == "dk"][:, 1, :], "T1", use)
                    elif kind == "dv":
                        take(dv[:, 1, :], "T1", use)
                    elif key == ("glu", 0):
                        dve.wait_ge(*st.at(unit_done, u + 1))
                        for j, bk in enumerate(b):
                            dve.wait_ge(*st.at(*freed(["T0", "T1"][j], ("glu", 1))))
                            tt(v_re_im[:, j, :], bank[bk][:, :], flat(sg[:, 2 * j:2 * j + 2, :])).then_inc(*st.sig(*freed(bk, key)))
                        for j in range(2):
                            dve.wait_ge(*st.at(glu_hi, j + 1))
                            tt(flat(hT_lo[:, 2 * j:2 * j + 2, :]), v_re_im[:, j, :],
                                      f32(flat(hT_hi[:, 2 * j:2 * j + 2, :])), ALU.subtract).then_inc(*st.sig(glu_ready))
                    elif kind == "branch":
                        cb, n = key[1:]
                        dve.wait_ge(*st.at(unit_done, u + 1))
                        dve.wait_ge(*st.at(gate_ready, {1: 1, 2: 2, 0: 3}[n]))
                        for j, bk in enumerate(b):
                            k0 = 4 * cb + 2 * j + (8 if n == 2 else 0)
                            g = flat((qk if n == 0 else gates)[:, k0:k0 + 2, :])
                            if n == 1:
                                tt(macc(cb, j), bank[bk][:, :], g).then_inc(*st.sig(*freed(bk, key)))
                                continue
                            tt(tmp[:, j, :], bank[bk][:, :], g).then_inc(*st.sig(*freed(bk, key)))
                        if n != 1:
                            dve.wait_ge(*st.mine())
                            for j in range(2):
                                ins = tt(macc(cb, j), macc(cb, j), tmp[:, j, :], ALU.add)
                                ins.then_inc(*st.sig(mg_made)) if n == 0 else ins.then_inc(*st.mid())
                            dve.wait_ge(*st.mine())
                        if n == 0:
                            for j in range(2):
                                dve.wait_ge(*st.at(mg_hi, 2 * cb + j + 1))
                                hi, lo = merged(cb)
                                tt(flat(lo[:, 2 * j:2 * j + 2, :]), macc(cb, j),
                                          f32(flat(hi[:, 2 * j:2 * j + 2, :])), ALU.subtract).then_inc(*st.sig(mg_ready))
                    elif kind in ("wout", "xo", "down"):
                        residual(key, b)
                    elif kind == "up":
                        g, i = key[1:]
                        dve.wait_ge(*st.at(*freed(b[0], key)))
                        tt(q_b[i], r_b[i], r_b[i]).then_inc(*st.sig(sq_made))
                        dve.wait_ge(*st.at(hid_hi, 2 * g + i + 1))
                        k0 = 4 * (g % 2) + 2 * i
                        tt(flat(bT_lo[:, k0:k0 + 2, :]), q_b[i], f32(flat(bT_hi[:, k0:k0 + 2, :])),
                                  ALU.subtract).then_inc(*st.sig(hid_ready))

                def stage(s):
                    kind = s[0]
                    if kind == "params":
                        params()
                    elif kind == "stats" and s[2]:
                        stats(s[1])
                    elif kind == "norm":
                        norm(s[1])
                    elif kind == "ssm_prep":
                        ssm_prep()
                    elif kind == "ssm_bt":
                        ssm_bt()
                    elif kind == "ssm_ct":
                        ssm_ct()
                    elif kind == "turn":
                        dve.wait_ge(*st.at(*full_at("X1", s)))
                        V.tensor_copy(flat(dT[:, 4 * s[1] + 2:4 * s[1] + 4, :]), bank["X1"][:, :]).then_inc(*st.sig(*freed("X1", s)))
                    elif kind == "sb_s":
                        h = s[1]
                        if h >= 2:
                            dve.wait_ge(*st.at(sbp_done, h - 1))
                        dve.wait_ge(*st.at(*full_at("X0", s)))
                        z = z_b[h % 2]
                        tt(z[:, 0:T], bank["X0"][:, 0:T], mask_s, ALU.min).then_inc(*st.mid())
                        tt(z[:, T:384], bank["X0"][:, T:384], mask_s[:, 0:P], ALU.min).then_inc(*st.sig(*freed("X0", s)))
                    elif kind == "sb_u":
                        z = z_b[s[1] % 2]
                        dve.wait_ge(*st.at(*full_at("X1", s)))
                        tt(z, z, bank["X1"][:, 0:384], ALU.subtract).then_inc(*st.sig(*freed("X1", s)))
                    elif kind == "sb_p" and s[1] % 2:
                        k = s[1] // 2
                        dve.wait_ge(*st.at(sb_hi, k + 1))
                        tt(bT_lo[:, 4 + k, :], bank["A3"][:, 0:T], f32(bT_hi[:, 4 + k, :]), ALU.subtract).then_inc(*st.sig(*freed("A3", ("sb_p", s[1] - 1))))
                    elif kind == "da_s":
                        j = s[1]
                        qt = j // DA_HEADS
                        nk = P * (qt + 1)
                        p = p_b[j % 2][:, :, 0:nk]
                        if j >= 2:
                            dve.wait_ge(*st.at(*full_at("X1", ("da_t", j - 2))))
                        for c, b in enumerate(("X0", "X1")):
                            dve.wait_ge(*st.at(*full_at(b, s)))
                            tt(p[:, c, :], bank[b][:, 0:nk], mask_n[:, T - nk:T], ALU.min).then_inc(*st.sig(*freed(b, s)))
                        dve.wait_ge(*st.mine())
                        V.tensor_reduce(DMX, p, AX.X, ALU.max).then_inc(*st.mid())
                        dve.wait_ge(*st.mine())
                        V.tensor_scalar(DNB[j % 2], DMX, -DSCALE, None, ALU.mult).then_inc(*st.sig(dmax_ready))
                    elif kind == "da_n":
                        qt = s[1]
                        o4 = o_b.rearrange("p (h n) -> p h n", n=P)
                        sq4 = att[:, 0:512].rearrange("p (h n) -> p h n", n=P)
                        dve.wait_ge(*st.at(dap_done, DA_HEADS * (qt + 1)))
                        V.tensor_copy(o_b, bank["A3"][:, :]).then_inc(*st.sig(*freed("A3", ("da_p", DA_HEADS * qt))))
                        dve.wait_ge(*st.mine())
                        tt(sq4, o4, o4).then_inc(*st.mid())
                        dve.wait_ge(*st.mine())
                        V.tensor_reduce(OSS, sq4, AX.X, ALU.add).then_inc(*st.sig(oss_ready))
                        dve.wait_ge(*st.at(o_r0, qt + 1))
                        newton(st, OR0, OSS, P, OVV, OTT, ORSTD)
                        tt(o4, o4, ORSTD.unsqueeze(2).broadcast_to([P, 4, P])).then_inc(*st.sig(on_ready))
                    elif kind == "da_o":
                        qt = s[1]
                        dve.wait_ge(*st.at(da_hi, qt + 1))
                        V.scalar_tensor_tensor(
                            out=bT_lo[:, 8:12, qt * P:qt * P + P], in0=bank["X1"][:, :].rearrange("p (h n) -> p h n", n=P),
                            scalar=GSUB, in1=f32(bT_hi[:, 8:12, qt * P:qt * P + P]), op0=ALU.mult, op1=ALU.subtract).then_inc(*st.sig(*freed("X1", s)))
                    elif kind == "gelu":
                        gl = v_re_im[:, :, :].rearrange("p r (k n) -> p (r k) n", n=T)
                        for k in range(KB):
                            dve.wait_ge(*st.at(gelu_hi, k + 1))
                            tt(bT_lo[:, k, :], gl[:, k, :], f32(bT_hi[:, k, :]), ALU.subtract).then_inc(*st.sig(gelu_ready))
                    elif kind == "memg":
                        for k in range(KD):
                            dve.wait_ge(*st.at(mem_hi, k + 1))
                            V.scalar_tensor_tensor(out=bT_lo[:, 4 + k, :], in0=memT[:, k, :],
                                                          scalar=col[:, R_MEM + k:R_MEM + k + 1],
                                                          in1=f32(bT_hi[:, 4 + k, :]), op0=ALU.mult, op1=ALU.subtract).then_inc(*st.sig(mem_ready))
                    elif kind == "xa_s":
                        h = s[1]
                        b = stage_banks(s)[0]
                        dve.wait_ge(*st.at(*full_at(b, s)))
                        V.tensor_reduce(DMX, bank[b][:, :].rearrange("p (t n) -> p t n", t=NT), AX.X, ALU.max).then_inc(*st.mid())
                        dve.wait_ge(*st.mine())
                        V.tensor_scalar(XNB[h], DMX, -XSCALE, None, ALU.mult).then_inc(*st.sig(xmax_ready))
                        dve.wait_ge(*st.mine())
                    elif kind == "xa_p":
                        h = s[1]
                        b = stage_banks(s)[0]
                        dve.wait_ge(*st.at(xo_hi, h + 1))
                        tt(bT_lo[:, h, :], bank[b][:, 0:T], f32(bT_hi[:, h, :]), ALU.subtract).then_inc(*st.sig(*freed(b, s)))

                def later(s):
                    kind = s[0]
                    if kind == "sb_s":
                        z, nl = z_b[s[1] % 2], nl_b[s[1] % 2]
                        dve.wait_ge(*st.at(ln_ready, s[1] + 1))
                        V.scalar_tensor_tensor(out=nl, in0=z, scalar=0.0, in1=nl, op0=ALU.max, op1=ALU.add)\
                         .then_inc(*st.sig(nl_ready))
                    elif kind == "da_s":
                        j = s[1]
                        nk = P * (j // DA_HEADS + 1)
                        p = p_b[j % 2]
                        dve.wait_ge(*st.at(dexp_ready, j + 1))
                        V.reciprocal(DRR, DRS[j % 2]).then_inc(*st.mid())
                        dve.wait_ge(*st.mine())
                        tt(DR2, DRR[:, 1:2], lam[:, 0:1]).then_inc(*st.mid())
                        V.tensor_scalar(p[:, 0, 0:nk], p[:, 0, 0:nk], DRR[:, 0:1], None, ALU.mult).then_inc(*st.mid())
                        dve.wait_ge(*st.mine())
                        V.scalar_tensor_tensor(out=p[:, 0, 0:nk], in0=p[:, 1, 0:nk], scalar=DR2,
                                                      in1=p[:, 0, 0:nk], op0=ALU.mult, op1=ALU.add).then_inc(*st.sig(dw_ready))
                    elif kind == "xa_s":
                        h = s[1]
                        dve.wait_ge(*st.at(*freed(stage_banks(("xa_s", h))[0], ("xa_s", h))))
                        V.reciprocal(DRR, XRS[h]).then_inc(*st.mid())
                        dve.wait_ge(*st.mine())
                        tt(e_b[h], e_b[h], DRR.unsqueeze(2).broadcast_to([P, NT, T])).then_inc(*st.sig(xw_ready))
                        dve.wait_ge(*st.mine())
                    elif kind == "ssm_in":
                        ssm_in(s[1])
                    elif kind == "ssm_rot":
                        ssm_rot(s[1])
                    elif kind == "ssm_out" and s[1] % 2:
                        k = s[1] // 2
                        dve.wait_ge(*st.at(s_used, s[1] + 1))
                        V.scalar_tensor_tensor(out=uT[:, k, :], in0=uT[:, k, :], scalar=col[:, R_D + k:R_D + k + 1],
                                                      in1=bank["A2"][:, 0:T], op0=ALU.mult, op1=ALU.add).then_inc(*st.sig(*freed("A2", ("ssm_out", s[1] - 1))))

                prep(0)
                prep(1)
                for u in range(-1, NU):
                    preps = 0 <= u < NU - HL
                    if preps and u not in STAGES_FIRST:
                        prep(u + HL)
                    if u >= 0:
                        evac(u)
                    for s in SIDE[u]:
                        dve.wait_ge(*st.mine())
                        stage(s)
                    if preps and u in STAGES_FIRST:
                        prep(u + HL)
                    for s in SIDE[u]:
                        dve.wait_ge(*st.mine())
                        later(s)
                dve.wait_ge(*st.mine())
            dve.wait_ge(end_act, 4)
            est = Steps(end_dve)
            newton(est, R0, SS, D, VV, TT, RSTD)
            dve.wait_ge(nf_landed, 16)
            for t in range(NT):
                V.scalar_tensor_tensor(out=xn[:, t, :], in0=x[:, t, :], scalar=RSTD[:, t:t + 1],
                                       in1=flat(uT[:, :, :]), op0=ALU.mult, op1=ALU.mult).then_inc(*est.mid())

        @block.tensor
        def _(pe):
            mm = nc.tensor.matmul

            def turn(o, i, n=P):
                return nc.tensor.transpose(o, i, ident[0:n, 0:n])

            pe.wait_ge(consts_made, 12)
            turn(bank["A0"][:, 0:P], gmaskT[:, :]).then_inc(pre_pe, 1)
            pe.wait_ge(pre_dve, 6)

            def turn_rows(b, j, src):
                for k in (0, 1):
                    for t in range(NT):
                        c = (2 * j + k) * P
                        ins = turn(bank[b][:, k * T + t * P:k * T + t * P + P], src[:, t, c:c + P])
                return ins

            def turn_scaled(b, j, src):
                for k in (0, 1):
                    for t in range(NT):
                        c = (2 * j + k) * P
                        ins = mm(bank[b][:, k * T + t * P:k * T + t * P + P], src[:, t, c:c + P], dg[t],
                                 start=True, stop=True)
                return ins

            for j, b in enumerate(NORM_BANKS):
                turn_scaled(b, j, xn).then_inc(pre_pe, 1)
            pe.wait_ge(pre_dve, 11)

            with pe.Fori(0, DEPTH) as l:
                st = Steps(None, l)

                def three(o, lhi, llo, rhi, rlo, first, last):
                    mm(o, lhi, rhi, start=first, stop=False)
                    mm(o, lhi, rlo, start=False, stop=False)
                    return mm(o, llo, rhi, start=False, stop=last)

                def sources(key):
                    kind = key[0]
                    if kind in ("xk",):
                        return bT_hi, bT_lo, 4
                    if kind == "xv":
                        return bT_hi, bT_lo, 4 + 4 * key[1]
                    if kind == "glu":
                        return bT_hi, bT_lo, 0
                    if kind == "branch":
                        return {0: (hT_hi, hT_lo, 0), 1: (bT_hi, bT_lo, 4), 2: (bT_hi, bT_lo, 8)}[key[2]]
                    if kind == "wout":
                        return (bT_hi, bT_lo, 0) if key[1] % 2 == 0 else (hT_hi, hT_lo, 4)
                    if kind == "xo":
                        return bT_hi, bT_lo, 0
                    if kind == "down":
                        return bT_hi, bT_lo, 4 * (key[1] % 2)
                    return hT_hi, hT_lo, 4 * (key[1] % 2) if kind in ("sv", "dq", "dk", "dv") else 0

                def inputs(key):
                    if key == ("glu", 1):
                        return [(gelu_ready, KB)]
                    if key == ("branch", 0, 1):
                        return [freed("A3", ("sb_p", SB_HEADS - 2))]
                    if key == ("branch", 0, 2):
                        return [freed("X1", ("da_o", 1))]
                    if key == ("branch", 0, 0):
                        return [(glu_ready, 2)]
                    if key == ("wout", 0):
                        return [(mg_ready, 2)]
                    if key == ("wout", 1):
                        return [(mg_ready, 4)]
                    if key == ("xk", 0):
                        return [(mem_ready, KD)]
                    if key == ("xo", 0):
                        return [freed(stage_banks(("xa_p", h))[0], ("xa_p", h)) for h in (2, 3)]
                    if key[0] == "down" and key[2] == 0:
                        return [(hid_ready, 2 * key[1] + 2)]
                    return []

                def unit(u):
                    key = KEYS[u]
                    mat, kind, kt, cols, k0, c0 = UNITS[u]
                    banks = unit_banks(key)
                    pe.wait_ge(*st.at(hi_made, u + 1))
                    pe.wait_ge(*st.at(lo_made, u + 1))
                    pe.wait_ge(*st.at(lo_made_pool, u + 1))
                    for w in inputs(key):
                        pe.wait_ge(*st.at(*w))
                    if opens(key):
                        for b in banks:
                            pe.wait_ge(*st.at(*before(b, ("down",) if key[0] == "down" else key)))
                    hi, lo, s0 = sources(key)
                    wh, wl = wslot(w_hi[u % HL], u), wslot(w_lo[u % HL], u)
                    after_norm = {("u", 0): "mix", ("xq", 0): "cross", ("up", 0, 0): "mlp"}.get(key)
                    if kind == "T":
                        for ft in range(cols // P):
                            o = bank[banks[ft // 2]][:, (ft % 2) * T:(ft % 2) * T + T]
                            for k in range(kt):
                                if after_norm and ft == 0 and k % 2 == 0:
                                    pe.wait_ge(*st.at(*freed(NORM_BANKS[k // 2], ("norm", after_norm))))
                                c = slice(ft * P, ft * P + P)
                                ins = three(o, wh[:, k, c], wl[:, k, c], hi[:, s0 + k, :], lo[:, s0 + k, :],
                                            k == 0, k == kt - 1)
                    else:
                        for t in range(NT):
                            for k in range(kt):
                                c = slice(t * P, t * P + P)
                                ins = three(bank[banks[t]][:, :], hi[:, s0 + k, c], lo[:, s0 + k, c], wh[:, k, :],
                                            wl[:, k, :], opens(key) and k == 0, closes(key) and k == kt - 1)
                    ins.then_inc(*st.sig(unit_done))

                def stage(s):
                    kind = s[0]
                    if kind == "params":
                        pe.wait_ge(*st.at(prm_landed, 9))
                        pe.wait_ge(*st.at(prm_spread, 1))
                        pe.wait_ge(*st.at(*before("X1", s)))
                        turn(bank["X1"][:, 0:R_END], prm[0:R_END, :], R_END).then_inc(*st.sig(full["X1"]))
                    elif kind == "norm":
                        pe.wait_ge(*st.at(diag_ready, NT * (NORMS.index(s[1]) + 1)))
                        for j, b in enumerate(NORM_BANKS):
                            pe.wait_ge(*st.at(*before(b, s)))
                            turn_scaled(b, j, x).then_inc(*st.sig(full[b]))
                    elif kind in ("ssm_bt", "ssm_ct"):
                        if kind == "ssm_bt":
                            pe.wait_ge(*st.at(b_ready, 1))
                        else:
                            pe.wait_ge(*st.at(mat_landed, 6))
                        src = bN if kind == "ssm_bt" else cN
                        for r, b in enumerate(stage_banks(s)):
                            pe.wait_ge(*st.at(*before(b, s)))
                            for k in range(4):
                                ins = turn(bank[b][:, k * P:k * P + P], src[:, r, k * P:k * P + P])
                            ins.then_inc(*st.sig(full[b]))
                    elif kind == "ssm_in":
                        i = s[1]
                        if i == 0:
                            pe.wait_ge(*st.at(*freed("A1", ("ssm_bt",))))
                            pe.wait_ge(*st.at(*freed("A3", ("ssm_ct",))))
                            pe.wait_ge(*st.at(*freed("T1", ("u", 1))))
                        for j, b in enumerate(("A0", "A1")):
                            pe.wait_ge(*st.at(*before(b, s)))
                            for r in range(2):
                                k, q = divmod(2 * i + j, 4)
                                ins = mm(bank[b][:, r * T:r * T + T], bt[32 * q:32 * q + 32, r, k, :],
                                         uT[32 * q:32 * q + 32, k, :], start=True, stop=True)
                            ins.then_inc(*st.sig(full[b]))
                    elif kind == "ssm_out":
                        i = s[1]
                        pe.wait_ge(*st.at(s_ready, i + 1))
                        if i % 2 == 0:
                            pe.wait_ge(*st.at(*before("A2", s)))
                        for j in range(2):
                            k, q = divmod(2 * i + j, 4)
                            o = bank["A2"][32 * q:32 * q + 32, 0:T]
                            for r in range(2):
                                ins = mm(o, ct[:, r, k, 32 * q:32 * q + 32], s_re_im[:, r, j * T:j * T + T],
                                         start=(r == 0), stop=(r == 1))
                        ins.then_inc(*st.sig(s_used))
                    elif kind == "turn":
                        w = s[1]
                        pe.wait_ge(*st.at(rope_done, w + 1))
                        for j, b in enumerate(("X0", "X1")):
                            pe.wait_ge(*st.at(*before(b, s)))
                            turn_rows(b, j, dN[w]).then_inc(*st.sig(full[b]))
                    elif kind == "sb_s":
                        h = s[1]
                        r, c = slice(HD * (h % 2), HD * (h % 2) + HD), h // 2
                        if h == 0:
                            for b, i in (("T0", 0), ("T1", 1)):
                                pe.wait_ge(*st.at(*freed(b, ("sk", i))))
                        pe.wait_ge(*st.at(*before("X0", s)))
                        mm(bank["X0"][:, 0:T], qk[r, 4 + c, 0:P], qk[r, c, :], start=True, stop=True)
                        mm(bank["X0"][:, T:T + P], qk[r, 4 + c, P:T], qk[r, c, P:T], start=True, stop=True).then_inc(*st.sig(full["X0"]))
                    elif kind == "sb_u":
                        nl = nl_b[s[1] % 2]
                        pe.wait_ge(*st.at(nl_ready, s[1] + 1))
                        pe.wait_ge(*st.at(*before("X1", s)))
                        o = bank["X1"]
                        mm(o[:, 0:384], tri[:, :], nl, start=True, stop=True)
                        mm(o[:, P:T], ones[:, :], nl[:, T:384], start=False, stop=True, skip_group_check=True).then_inc(*st.sig(full["X1"]))
                    elif kind == "sb_p":
                        h = s[1]
                        w = z_b[h % 2]
                        pe.wait_ge(*st.at(w_ready, h + 1))
                        if h == 0:
                            pe.wait_ge(*st.at(*freed("T0", ("sv", 0))))
                            pe.wait_ge(*st.at(*freed("T1", ("sv", 0))))
                        if h % 2 == 0:
                            pe.wait_ge(*st.at(*before("A3", s)))
                        r = slice(HD * (h % 2), HD * (h % 2) + HD)
                        c = slice(HD * h, HD * h + HD)
                        mm(bank["A3"][r, 0:T], vN[:, 0, c], w[:, 0:T], start=True, stop=True, skip_group_check=True)
                        mm(bank["A3"][r, P:T], vN[:, 1, c], w[:, T:384], start=False, stop=True, skip_group_check=True)\
                            .then_inc(*st.sig(sbp_done))
                    elif kind == "da_s":
                        qt, h = divmod(s[1], DA_HEADS)
                        nk = P * (qt + 1)
                        for c, b in enumerate(("X0", "X1")):
                            pe.wait_ge(*st.at(*before(b, s)))
                            r = slice(HD * c, HD * c + HD)
                            mm(bank[b][:, 0:nk], dT[r, h, qt * P:qt * P + P], dT[r, 4 + h, 0:nk],
                                    start=True, stop=True).then_inc(*st.sig(full[b]))
                    elif kind == "da_t":
                        j = s[1]
                        pe.wait_ge(*st.at(dw_ready, j + 1))
                        pe.wait_ge(*st.at(*before("X1", s)))
                        for kb in range(j // DA_HEADS + 1):
                            ins = turn(bank["X1"][:, kb * P:kb * P + P], p_b[j % 2][:, 0, kb * P:kb * P + P])
                        ins.then_inc(*st.sig(full["X1"]))
                    elif kind == "da_p":
                        qt, h = divmod(s[1], DA_HEADS)
                        pe.wait_ge(*st.at(*freed("X1", ("da_t", s[1]))))
                        if s[1] == 0:
                            pe.wait_ge(*st.at(*freed("T0", ("dv", 0))))
                            pe.wait_ge(*st.at(*freed("T1", ("dv", 0))))
                        if h == 0:
                            pe.wait_ge(*st.at(*before("A3", s)))
                        for kb in range(qt + 1):
                            ins = mm(bank["A3"][:, h * P:h * P + P], pT_b[s[1] % 2][:, kb * P:kb * P + P],
                                     dv[:, kb, h * P:h * P + P], start=(kb == 0), stop=(kb == qt))
                        ins.then_inc(*st.sig(dap_done))
                    elif kind == "da_o":
                        pe.wait_ge(*st.at(on_ready, s[1] + 1))
                        pe.wait_ge(*st.at(*before("X1", s)))
                        for h in range(DA_HEADS):
                            ins = turn(bank["X1"][:, h * P:h * P + P], o_b[:, h * P:h * P + P])
                        ins.then_inc(*st.sig(full["X1"]))
                    elif kind == "xa_s":
                        h = s[1]
                        b = stage_banks(s)[0]
                        if h % 2 == 0:
                            pe.wait_ge(*st.at(*freed(f"T{h // 2}", ("xq", h // 2))))
                        pe.wait_ge(*st.at(*before(b, s)))
                        for qt in range(NT):
                            ins = mm(bank[b][:, qt * T:qt * T + T], qk[:, h, qt * P:qt * P + P], qk[:, 4 + h, :],
                                     start=True, stop=True)
                        ins.then_inc(*st.sig(full[b]))
                    elif kind == "xa_t":
                        h = s[1]
                        b = stage_banks(s)[0]
                        pe.wait_ge(*st.at(xw_ready, h + 1))
                        pe.wait_ge(*st.at(*before(b, s)))
                        for mt in range(2):
                            for qt in range(NT):
                                ins = turn(bank[b][:, mt * T + qt * P:mt * T + qt * P + P],
                                           e_b[h][:, qt, mt * P:mt * P + P])
                        ins.then_inc(*st.sig(full[b]))
                    elif kind == "xa_p":
                        h = s[1]
                        b = stage_banks(s)[0]
                        tb = stage_banks(("xa_t", h))[0]
                        pe.wait_ge(*st.at(*freed(tb, ("xa_t", h))))
                        if h == 0:
                            pe.wait_ge(*st.at(*freed("T0", ("xv", 0))))
                            pe.wait_ge(*st.at(*freed("T1", ("xv", 0))))
                        pe.wait_ge(*st.at(*before(b, s)))
                        for mt in range(2):
                            ins = mm(bank[b][:, 0:T], vN[:, mt, h * P:h * P + P], eT_b[h][:, mt, :],
                                     start=(mt == 0), stop=(mt == 1))
                        ins.then_inc(*st.sig(full[b]))

                for u in range(-1, NU):
                    if u >= 0:
                        unit(u)
                    for s in SIDE[u]:
                        stage(s)

    bad = [(s.name, s.made, s.per_layer) for s in signals if s.made != s.per_layer]
    assert not bad, bad


_INS = ["x", "mem", "positions", "norm_mix", "w_in", "ssm_lam_re", "ssm_lam_im", "ssm_log_dt", "ssm_b_re", "ssm_b_im",
        "ssm_c_re", "ssm_c_im", "ssm_d", "ssm_w_glu", "diff_lambda", "diff_subln", "w_branch", "w_out", "norm_cross",
        "norm_mem", "w_xq", "w_xkv", "w_xo", "norm_mlp", "w_up", "w_down", "norm_final"]


def kernel(**inputs):
    import numpy as _np
    import concourse.bacc as _bacc
    from concourse.bass_utils import run_bass_kernel_spmd as _run

    nc = _bacc.Bacc("TRN2", target_bir_lowering=False, num_devices=1)
    arrays, args = {}, {}
    for name in _INS:
        v = _np.ascontiguousarray(inputs[name])
        arrays[f"in_{name}"] = v
        args[name] = nc.dram_tensor(f"in_{name}", v.shape, mybir.dt.from_np(v.dtype), kind="ExternalInput").ap()
    out = nc.dram_tensor("out_0", (1, T, D), F32, kind="ExternalOutput").ap()
    hybrid_trunk(nc, args, out)
    r = _run(nc, [arrays], core_ids=[0])
    return r.results[0]["out_0"]
```

```python
import math
from contextlib import ExitStack

import numpy as np

import concourse.bass as bass
from concourse import mybir

ALU = mybir.AluOpType
ACT = mybir.ActivationFunctionType
AX = mybir.AxisListType
F32 = mybir.dt.float32
F32R = mybir.dt.float32r
I32 = mybir.dt.int32

P = 128
DEPTH, D, T = 2, 1024, 256
NT = T // P
KD = D // P
BW = 512
KB = BW // P
HIDDEN = 4 * D
SB_HEADS, HD = 8, 64
DA_HEADS = 4
XA_HEADS = 4
ROT, ROT_HALF = 16, 8
ROPE_THETA = 500000.0
RMS_EPS = 1e-6
GROUPS, GC, STATES = 32, 16, 64
STILES = GROUPS * STATES // P
SSM_STEPS = STILES // 2
BIG, NEG = 3.0e38, -1.0e30
TWO_PI = 2 * math.pi
PI_HI = float(np.float32(6.28125))
PI_MID = float(np.float32(TWO_PI - 6.28125))
PI_LO = float(np.float32(TWO_PI - 6.28125 - float(np.float32(TWO_PI - 6.28125))))
PI_SAFE = float(np.nextafter(np.float32(math.pi), np.float32(0)))
ROUND = 1.5 * 2.0 ** 23

UW = 2048
RAW, HL = 2, 3


def pool_cols(u):
    return 128 if 3 <= u < 9 else 640


R_MIX, R_CROSS, R_MEM, R_MLP, R_D, R_SUBLN, R_LRE, R_LIM, R_DT, R_END = 0, 8, 16, 24, 32, 36, 37, 53, 96, 112


def plan():
    units, name = [], {}

    def add(key, *u):
        name[key] = len(units)
        units.append(u)

    def wide(key, mat, kind, c0, n=2):
        for i in range(n):
            if kind == "T":
                add((key, i), mat, "T", KD, 256, 0, c0 + 256 * i)
            else:
                add((key, i), mat, "N", 4, 512, 4 * (i % 2), c0 + 512 * (i // 2))

    wide("u", "w_in", "T", 0)
    wide("sq", "w_in", "T", 512)
    wide("sk", "w_in", "T", 1024)
    wide("sv", "w_in", "N", 1536)
    wide("dq", "w_in", "N", 2048)
    wide("dk", "w_in", "N", 2560)
    wide("dv", "w_in", "N", 3072)
    for n in (1, 2, 0):
        wide(("gate", n), "w_in", "T", 3584 + D * n, 4)
    add(("glu", 1), "ssm_w_glu", "T", KB, 512, 0, 512)
    add(("glu", 0), "ssm_w_glu", "T", KB, 512, 0, 0)
    for cb in range(2):
        for n in (1, 2, 0):
            add(("branch", cb, n), ("w_branch", n), "T", KB, 512, 0, 512 * cb)
    wide("wout", "w_out", "N", 0, 4)
    wide("xk", "w_xkv", "T", 0)
    wide("xq", "w_xq", "T", 0)
    wide("xv", "w_xkv", "N", BW)
    for cb in range(2):
        add(("xo", cb), "w_xo", "N", 4, 512, 0, 512 * cb)

    def up(g):
        for i in range(2):
            add(("up", g, i), "w_up", "T", KD, 256, 0, 512 * g + 256 * i)

    def down(g):
        for cb in range(2):
            add(("down", g, cb), "w_down", "N", 4, 512, 4 * g, 512 * cb)

    groups = HIDDEN // 512
    up(0)
    for g in range(1, groups):
        up(g)
        down(g - 1)
    down(groups - 1)
    return units, name


UNITS, AT_UNIT = plan()
NU = len(UNITS)
assert NU % RAW == 0 and NU % HL == 0


def side_stages():
    side = {u: [] for u in range(-1, NU)}

    def after(u, *stage):
        side[u].append(stage)

    after(-1, "spread")
    after(-1, "turn_x", "mix", 0)
    after(-1, "turn_x", "mix", 1)
    after(-1, "params")
    after(-1, "stats", "mix", 0)
    after(-1, "stats", "mix", 1)
    after(-1, "norm", "mix")
    after(0, "ssm_angle")
    after(1, "ssm_f")
    for k in range(8):
        after(2 + k // 2, "ssm_pow", k)
    after(6, "ssm_rot0")
    after(2, "ssm_ct")
    after(3, "ssm_b")
    after(5, "ssm_bt")
    for h in range(SB_HEADS):
        after(6 + h, "sb_s", h)
        after(7 + h, "sb_u", h)
        after(8 + h, "sb_p", h)
    after(10, "rope", 0)
    after(14, "turn", 0)
    after(12, "rope", 1)
    after(15, "turn", 1)
    for i in range(SSM_STEPS):
        after(7 + 2 * i, "ssm_in", i)
        after(8 + 2 * i, "ssm_rot", i)
        after(9 + 2 * i, "ssm_out", i)
    after(23, "gelu")
    for j in range(2 * DA_HEADS):
        after(16 + j, "da_s", j)
        after(17 + j, "da_t", j)
        after(18 + j, "da_p", j)
    after(21, "da_n", 0)
    after(23, "da_o", 0)
    after(25, "da_n", 1)
    after(27, "da_o", 1)
    after(33, "memg")
    after(AT_UNIT["wout", 1], "stats", "cross", 0)
    after(AT_UNIT["wout", 3], "stats", "cross", 1)
    after(AT_UNIT["wout", 3], "turn_x", "cross", 0)
    after(AT_UNIT["xk", 0], "turn_x", "cross", 1)
    after(AT_UNIT["xk", 0], "norm", "cross")
    xq = AT_UNIT["xq", 0]
    for h in range(XA_HEADS):
        after(xq + h // 2, "xa_s", h)
        after(xq + 1 + h // 2, "xa_t", h)
    for h in range(XA_HEADS):
        after(xq + h // 2, "xa_w", h)
    for h in range(XA_HEADS):
        after(xq + 3, "xa_p", h)
    after(AT_UNIT["xo", 0], "stats", "mlp", 0)
    after(AT_UNIT["xo", 1], "turn_x", "mlp", 0)
    after(AT_UNIT["xo", 1], "turn_x", "mlp", 1)
    after(AT_UNIT["xo", 1], "stats", "mlp", 1)
    after(AT_UNIT["xo", 1], "norm", "mlp")
    return side


SIDE = side_stages()
ACT_PREP_EARLY = set(range(0, 16)) | set(range(AT_UNIT["up", 0, 0], NU))
DVE_PREP_EARLY = set(range(0, 5)) | set(range(AT_UNIT["up", 0, 0], NU))
PREP_BEFORE_EVAC = set(range(AT_UNIT["up", 0, 0], NU))
_RANK = {"sb_p": 0, "da_p": 0, "sb_u": 1, "da_t": -1, "sb_s": 2, "da_s": 2, "da_o": -1, "da_n": 3, "ssm_in": 4, "ssm_rot": 5,
         "ssm_out": 6}
for _u in range(7, 27):
    SIDE[_u].sort(key=lambda s: _RANK.get(s[0], 7))


def unit_banks(key):
    if key[0] in ("u", "sq", "sk", "xk", "xq") or isinstance(key[0], tuple):
        return ["T0", "T1"][key[1] % 2:][:1]
    if key[0] in ("sv", "dq", "dk", "dv", "xv"):
        return ["T0", "T1"]
    if key[0] == "glu":
        return ["T0", "T1"] if key[1] else ["A0", "A1"]
    if key[0] == "branch":
        return {1: ["T0", "T1"], 2: ["A0", "A1"], 0: ["A2", "A3"]}[key[2]]
    if key[0] == "wout":
        return ["A0", "A1"] if key[1] < 2 else ["A2", "A3"]
    if key[0] == "xo":
        return ["A2", "A3"] if key[1] == 0 else ["A0", "A1"]
    if key[0] == "up":
        return ["T0", "T1"][key[2]:][:1]
    return ["A0", "A1"] if key[2] == 0 else ["A2", "A3"]


def opens(key):
    if key[0] in ("sv", "dq", "dk", "dv", "xv"):
        return key[1] == 0
    if key[0] == "wout":
        return key[1] % 2 == 0
    if key[0] == "down":
        return key[1] == 0
    return True


def closes(key):
    if key[0] in ("sv", "dq", "dk", "dv", "xv"):
        return key[1] == 1
    if key[0] == "wout":
        return key[1] % 2 == 1
    if key[0] == "down":
        return key[1] == HIDDEN // 512 - 1
    return True


TURN_BANKS = ["X0", "X1", "A2", "A3"]


def stage_banks(s):
    return {
        "params": ["T0"], "norm": ["A1"], "ssm_bt": ["A0", "A1"], "ssm_ct": ["A2", "A3"],
        "sb_s": ["X0"], "sb_u": ["X1"], "turn": ["X0", "X1"], "ssm_in": ["A0", "A1"],
        "da_s": ["X0", "X1"], "da_t": ["X1"], "da_o": ["X1"],
    }.get(s[0]) or (
        TURN_BANKS[2 * s[2]:2 * s[2] + 2] if s[0] == "turn_x" else
        ["A3"] if s[0] == "sb_p" and s[1] % 2 == 0 else
        ["A2"] if s[0] == "ssm_out" and s[1] % 2 == 0 else
        ["A3"] if s[0] == "da_p" and s[1] % 4 == 0 else
        [["X0", "A0", "A1", "A2"][s[1]]] if s[0] == "xa_s" else
        [["X1", "X0"][s[1] % 2]] if s[0] == "xa_t" else
        [["A0", "A1", "A3", "A2"][s[1]]] if s[0] == "xa_p" else [])


KEYS = [None] * NU
for _k, _i in AT_UNIT.items():
    KEYS[_i] = _k
BANKS = ["A0", "A1", "A2", "A3", "T0", "T1", "X0", "X1"]
USES = {b: [] for b in BANKS}
for _u in range(-1, NU):
    if _u >= 0 and opens(KEYS[_u]):
        for _b in unit_banks(KEYS[_u]):
            USES[_b].append(KEYS[_u] if KEYS[_u][0] != "down" else ("down",))
    for _s in SIDE[_u]:
        for _b in stage_banks(_s):
            USES[_b].append(_s)
OWN_SIGNAL = ("ssm_out", "sb_p", "da_p")
FULLS = {b: [k for k in USES[b] if not (k in AT_UNIT or k == ("down",) or k[0] in OWN_SIGNAL)] for b in BANKS}


class Signal:

    def __init__(self, ctx, nc, name, per_layer, credit=0, step=1):
        self.sem = ctx.enter_context(nc.semaphore(name))
        self.name, self.per_layer, self.credit, self.step, self.made = name, per_layer, credit, step, 0

    def value(self, layer, n):
        return layer * (self.per_layer * self.step) + (n * self.step + self.credit)


class Steps:

    def __init__(self, order, layer=None):
        self.order, self.n, self.last, self.layer = order, 0, None, layer

    def mid(self):
        self.n += 1
        self.last = (self.order, self.n)
        return self.order, 1

    def sig(self, signal, n=None):
        signal.made += 1
        self.last = (signal.sem, signal.value(self.layer, signal.made if n is None else n))
        return signal.sem, 1

    def mark(self, milestones):
        milestones.n += 1
        self.last = (milestones.order, milestones.n)
        return milestones.order, 1

    def at(self, signal, n):
        return signal.sem, signal.value(self.layer, n)

    def mine(self):
        return self.last


def hybrid_trunk(nc, a, out):
    with ExitStack() as ctx:
        def sb(name, shape, dt=F32):
            return ctx.enter_context(nc.sbuf_tensor("s_" + name, shape, dt))

        def sem(name):
            return ctx.enter_context(nc.semaphore(name))

        def signal(name, per_layer, credit=0, step=1):
            s = Signal(ctx, nc, name, per_layer, credit, step)
            signals.append(s)
            return s

        signals = []

        raw = [sb(f"raw{i}", [P, UW]) for i in range(RAW)]
        w_lo = [sb(f"w_lo{i}", [P, UW], F32R) for i in range(HL)]
        w_hi = [sb(f"w_hi{i}", [P, UW], F32R) for i in range(HL)]
        x = sb("x", [P, NT, D])
        memT = sb("memT", [P, KD, T])
        hT_hi, hT_lo = sb("hT_hi", [P, KD, T], F32R), sb("hT_lo", [P, KD, T], F32R)
        bT_hi, bT_lo = sb("bT_hi", [P, 12, T], F32R), sb("bT_lo", [P, 12, T], F32R)
        gates = sb("gates", [P, 16, T])
        qk = sb("qk", [P, KD, T])
        uT = sb("uT", [P, KB, T])
        vN = sb("vN", [P, NT, BW])
        gates0 = [vN[:, :, :].rearrange("p t (k n) -> p (t k) n", n=T), qk[:, 4:8, :]]
        dT = qk
        dv = sb("dv", [P, NT, BW])
        bt = sb("bt", [P, 2, 4, P])
        ct = sb("ct", [P, 2, 4, P])
        pw1 = sb("pw1", [P, 2, STILES, 16])
        pw16 = sb("pw16", [P, 2, STILES, 16])
        rot = sb("rot", [P, 2, 2, 512])
        v_re_im = sb("v_re_im", [P, 2, 512])
        s_re_im = sb("s_re_im", [P, 2, 512])
        tmp = sb("tmp", [P, 2, 512])
        ptmp = sb("ptmp", [P, 512])
        att = sb("att", [P, 2560])
        masks = sb("masks", [P, 3 * P])
        mask_s = masks[:, 0:2 * P]
        mask_n = masks[:, P:3 * P]
        tri = sb("tri", [P, P])
        ones = sb("ones", [P, P])
        ident = sb("ident", [P, P])
        gmask = sb("gmask", [P, P])
        gmaskT = sb("gmaskT", [P, P])
        prm = sb("prm", [P, P])
        ldt = sb("ldt", [P, 2])
        eps = sb("eps", [P, 2])
        col = sb("col", [P, R_END])
        small = sb("small", [P, 24, STILES])
        stat = sb("stat", [P, 64])
        rope = sb("rope", [P, 2, NT, ROT_HALF])
        lam_all = sb("lam_all", [P, 2, DEPTH])
        lam = sb("lam", [P, 2])

        h_buf = gates[:, 0:8, :]
        xn = gates[:, 0:8, :].rearrange("p (t k) n -> p t (k n)", t=NT)
        dN = [gates[:, 8 + 4 * i:12 + 4 * i, :].rearrange("p (t k) n -> p t (k n)", t=NT) for i in range(2)]
        bN = gates[:, 0:4, :].rearrange("p (r k) n -> p r (k n)", r=2)
        cN = gates[:, 4:8, :].rearrange("p (r k) n -> p r (k n)", r=2)
        b_raw = s_re_im[:, :, 0:256]
        sg = s_re_im[:, :, :].rearrange("p r (k n) -> p (r k) n", n=T)
        z_b = [att[:, 768 * i:768 * i + 384] for i in range(2)]
        nl_b = [att[:, 768 * i + 384:768 * i + 768] for i in range(2)]
        p_b = [att[:, 1536 + 512 * i:2048 + 512 * i].rearrange("p (c n) -> p c n", c=2) for i in range(2)]
        pT_b = [att[:, 1024 + 256 * i:1280 + 256 * i] for i in range(2)]
        o_b = att[:, 512:1024]
        squares = [att[:, 2048:2560], ptmp[:, :]]
        e_b = [rot[:, h // 2, h % 2, :].rearrange("p (t n) -> p t n", t=NT) for h in range(XA_HEADS)]
        def merged(cb):
            return (bT_hi[:, 0:4, :], bT_lo[:, 0:4, :]) if cb == 0 else (hT_hi[:, 4:8, :], hT_lo[:, 4:8, :])

        def macc(cb, j):
            return rot[:, cb, j, :]

        eT_b = [att[:, 512 * i:512 * i + 512].rearrange("p (m n) -> p m n", m=2) for i in range(XA_HEADS)]
        r_b = [att[:, 512 * i:512 * i + 512] for i in range(2)]
        q_b = [att[:, 1024 + 512 * i:1536 + 512 * i] for i in range(2)]

        bank = {b: ctx.enter_context(nc.psum_tensor("p_" + b, [P, 512], F32)) for b in BANKS}
        full = {b: signal(f"{b}_full", len(FULLS[b])) for b in BANKS}
        free = {b: signal(f"{b}_free", len(USES[b]), credit=1) for b in BANKS}

        raw_landed = [signal(f"raw{i}_landed", NU // RAW, step=16) for i in range(RAW)]
        hi_made = signal("w_hi_made", NU, credit=RAW)
        lo_made = signal("w_lo_made", NU, credit=RAW)
        lo_made_pool = signal("w_lo_made_pool", NU, credit=RAW)
        unit_done = signal("unit_done", NU, credit=HL)
        prm_landed = signal("prm_landed", 9, step=16)
        mat_landed = signal("mat_landed", 6, step=16)
        prm_spread = signal("prm_spread", 1)
        prm_read = signal("prm_read", 1, credit=1)
        norm_r0 = signal("norm_r0", 3)
        norm_ss = signal("norm_ss", 3 * NT * 2)
        diag_ready = signal("diag_ready", 3 * NT)
        norm_hi = signal("norm_hi", 3 * KD)
        h_ready = signal("h_ready", 3 * KD // 2)
        dt_ready, lam_dt = signal("dt_ready", 1), signal("lam_dt", 1)
        decay_ready, angle_ready = signal("decay_ready", 1), signal("angle_ready", 1)
        cs_ready, b_ready = signal("cs_ready", 1), signal("b_ready", 1)
        rot_ready = signal("rot_ready", SSM_STEPS)
        rot_used = signal("rot_used", SSM_STEPS, credit=2)
        s_ready = signal("s_ready", SSM_STEPS)
        v_ready = signal("v_ready", SSM_STEPS)
        s_im_ready = signal("s_im_ready", SSM_STEPS)
        s_used = signal("s_used", SSM_STEPS, credit=1)
        gelu_hi, gelu_ready = signal("gelu_hi", KB), signal("gelu_ready", KB)
        rope_done = signal("rope_done", 2)
        ln_ready, nl_ready = signal("ln_ready", SB_HEADS), signal("nl_ready", SB_HEADS)
        w_ready, sbp_done = signal("w_ready", SB_HEADS), signal("sbp_done", SB_HEADS)
        sb_hi = signal("sb_hi", SB_HEADS // 2)
        NJ = NT * DA_HEADS
        dmax_ready, dexp_ready = signal("dmax_ready", NJ), signal("dexp_ready", NJ)
        dw_ready, dap_done = signal("dw_ready", NJ), signal("dap_done", NJ)
        oss_ready, o_r0, on_ready = signal("oss_ready", NT), signal("o_r0", NT), signal("on_ready", NT)
        da_hi = signal("da_hi", NT)
        glu_hi, glu_ready = signal("glu_hi", 2), signal("glu_ready", 2)
        gate_ready = signal("gate_ready", 4)
        mg_made, mg_hi, mg_ready = signal("mg_made", 4), signal("mg_hi", 4), signal("mg_ready", 4)
        mem_hi, mem_ready = signal("mem_hi", KD), signal("mem_ready", KD)
        xmax_ready, xw_ready = signal("xmax_ready", XA_HEADS), signal("xw_ready", XA_HEADS)
        xo_hi = signal("xo_hi", XA_HEADS)
        NUP = 2 * (HIDDEN // 512)
        sq_made, hid_hi, hid_ready = signal("sq_made", NUP), signal("hid_hi", NUP), signal("hid_ready", NUP)

        act_order, dve_order, pool_order = sem("act_order"), sem("dve_order"), sem("pool_order")
        x_landed, mem_landed, pos_landed, lam_landed = sem("x_landed"), sem("mem_landed"), sem("pos_landed"), sem("lam_landed")
        sp_held = sem("sp_held")
        nf_landed, stored = sem("nf_landed"), sem("stored")
        consts_made = sem("consts_made")
        pre_pe, pre_act, pre_dve = sem("pre_pe"), sem("pre_act"), sem("pre_dve")
        end_act, end_dve = sem("end_act"), sem("end_dve")

        def full_at(b, stage):
            return full[b], FULLS[b].index(stage) + 1

        def before(b, use):
            return free[b], USES[b].index(use)

        def freed(b, use):
            return free[b], USES[b].index(use) + 1

        def weight_src(u, l):
            mat, kind, kt, cols, k0, c0 = UNITS[u]
            m = a["w_branch"][l, mat[1]] if isinstance(mat, tuple) else a[mat][l]
            return m.rearrange("(k p) n -> p k n", p=P)[:, k0:k0 + kt, c0:c0 + cols]

        def wslot(tile, u):
            return tile[:, :].rearrange("p (k n) -> p k n", k=UNITS[u][2])

        def f32(ap):
            return ap.bitcast(F32)

        gain_row = {"mix": R_MIX, "cross": R_CROSS, "mlp": R_MLP}
        NORMS = ["mix", "cross", "mlp"]
        SS, R0, VV, TT, RSTD = (stat[:, 2 * i:2 * i + 2] for i in range(5))
        SS1, SS0V = stat[:, 36:38], stat[:, 38:40]
        r_row = tmp[:, 1, 0:T]
        dg = [tmp[:, 0, t * P:t * P + P] for t in range(NT)]
        DNB = [stat[:, 10 + 2 * i:12 + 2 * i] for i in range(2)]
        DMX = stat[:, 14:16]
        DRS = [stat[:, 16 + 2 * i:18 + 2 * i] for i in range(2)]
        DRR, DR2 = stat[:, 20:22], stat[:, 22:23]
        XRS = [stat[:, 24 + 2 * i:26 + 2 * i] for i in range(XA_HEADS)]
        XNB = [stat[:, 32 + 2 * i:34 + 2 * i] for i in range(XA_HEADS)]
        OSS, OR0, OVV, OTT, ORSTD = (stat[:, 40 + 4 * i:44 + 4 * i] for i in range(5))
        GSUB = stat[:, 60:61]
        XSCALE, DSCALE = float(P) ** -0.5, float(HD) ** -0.5
        DT, LD, TH, DECAY, KK, THR, THA, SIN, COS, LBR, LBI, DEN, T1, T2, FR, FI = (small[:, i, :] for i in range(16))

        def norm_input(which, half, t):
            if which == "mix":
                return free[f"A{2 * half + t}"], 0
            if which == "cross":
                return freed(f"A{2 * half + t}", ("wout", 2 * half))
            return freed(f"A{2 * (1 - half) + t}", ("xo", half))

        def x_part(t, key):
            cb = {"wout": lambda: key[1] // 2, "xo": lambda: key[1], "down": lambda: key[2]}[key[0]]()
            return x[:, t, 512 * cb:512 * cb + 512]

        block = ctx.enter_context(nc.Block())

        @block.sync
        def _(sp):
            sp.dma_start(xn, a["mem"][0].rearrange("(t p) d -> p t d", p=P)).then_inc(mem_landed, 16)
            sp.dma_start(x[:, :, :], a["x"][0].rearrange("(t p) d -> p t d", p=P)).then_inc(x_landed, 16)
            sp.wait_ge(consts_made, 1)
            with sp.Fori(0, DEPTH) as l:
                st = Steps(None, l)

                def load(dst, src, landed):
                    landed.made += 1
                    sp.dma_start(dst, src).then_inc(landed.sem, 16)

                def load_unit(u):
                    sp.wait_ge(*st.at(hi_made, u - RAW + 1))
                    sp.sem_inc(sp_held, 1)
                    sp.wait_ge(*st.at(lo_made, u - RAW + 1))
                    sp.sem_inc(sp_held, 1)
                    sp.wait_ge(*st.at(lo_made_pool, u - RAW + 1))
                    sp.sem_inc(sp_held, 1)
                    load(wslot(raw[u % RAW], u), weight_src(u, l), raw_landed[u % RAW])

                load_unit(0)
                sp.wait_ge(*st.at(prm_read, 0))
                sp.sem_inc(sp_held, 1)
                for r, name, rows in ((R_MIX, "norm_mix", KD), (R_CROSS, "norm_cross", KD), (R_MEM, "norm_mem", KD),
                                      (R_MLP, "norm_mlp", KD), (R_D, "ssm_d", KB), (R_SUBLN, "diff_subln", 1)):
                    load(prm[r:r + rows, :], a[name][l].rearrange("(r n) -> r n", n=P), prm_landed)
                load(prm[R_LRE:R_LRE + 16, :], a["ssm_lam_re"][l].rearrange("(i g) s -> i (g s)", g=2), prm_landed)
                load(prm[R_LIM:R_LIM + 16, :], a["ssm_lam_im"][l].rearrange("(i g) s -> i (g s)", g=2), prm_landed)
                load(ldt[R_DT:R_DT + 16, :], a["ssm_log_dt"][l].rearrange("(i g) -> i g", g=2), prm_landed)
                for u in range(1, NU):
                    load_unit(u)
                    if u == 4:
                        sp.wait_ge(*st.at(h_ready, KD // 2))
                        sp.sem_inc(sp_held, 1)
                        for r, nm in enumerate(("ssm_b_re", "ssm_b_im")):
                            load(b_raw[:, r, :].rearrange("p (i c) -> p i c", c=GC),
                                 a[nm][l].rearrange("(i g) s c -> (g s) i c", g=2), mat_landed)
                        for r, nm in enumerate(("ssm_c_re", "ssm_c_im")):
                            for half in range(2):
                                load(cN[:, r, :].rearrange("p (k h s) -> p k h s", h=2, s=STATES)[:, :, half, :],
                                     a[nm][l].rearrange("(k g) c s -> (g c) k s", g=8), mat_landed)
            sp.wait_ge(unit_done.sem, unit_done.value(DEPTH - 1, AT_UNIT["up", 2, 0]))
            sp.dma_start(uT[:, :, :].rearrange("p k n -> p (k n)"), a["norm_final"].partition_broadcast(P))\
              .then_inc(nf_landed, 16)
            for t in range(NT):
                sp.wait_ge(end_dve, 7 + t)
                sp.dma_start(out[0].rearrange("(t p) d -> p t d", p=P)[:, t, :], xn[:, t, :]).then_inc(stored, 16)
            sp.wait_ge(stored, 16 * NT)

        @block.gpsimd
        def _(pool):
            for s in signals:
                if s.credit:
                    pool.sem_inc(s.sem, s.credit)
            cst = Steps(consts_made)
            nc.gpsimd.memset(prm[:, :], 0.0).then_inc(*cst.mid())
            nc.gpsimd.memset(ident[:, :], 0.0).then_inc(*cst.mid())
            nc.gpsimd.memset(tri[:, :], 1.0).then_inc(*cst.mid())
            nc.gpsimd.memset(ones[:, :], 1.0).then_inc(*cst.mid())
            nc.gpsimd.memset(masks[:, :], BIG).then_inc(*cst.mid())
            nc.gpsimd.memset(gmaskT[:, :], 0.0).then_inc(*cst.mid())
            pool.wait_ge(*cst.mine())
            nc.gpsimd.affine_select(out=ident[:, :], in_=ident[:, :], compare_op=ALU.not_equal, fill=1.0, base=0,
                                          pattern=[[-1, P]], channel_multiplier=1).then_inc(*cst.mid())
            nc.gpsimd.affine_select(out=tri[:, :], in_=tri[:, :], compare_op=ALU.is_ge, fill=0.0, base=0,
                                          pattern=[[-1, P]], channel_multiplier=1).then_inc(*cst.mid())
            nc.gpsimd.affine_select(out=mask_s[:, 0:P], in_=mask_s[:, 0:P], compare_op=ALU.is_ge,
                                          fill=NEG, base=-1, pattern=[[1, P]], channel_multiplier=-1).then_inc(*cst.mid())
            nc.gpsimd.affine_select(out=mask_n[:, P:T], in_=mask_n[:, P:T], compare_op=ALU.is_ge, fill=NEG,
                                          base=0, pattern=[[-1, P]], channel_multiplier=1).then_inc(*cst.mid())
            for half in range(2):
                pool.wait_ge(*cst.mine())
                nc.gpsimd.memset(gmaskT[64 * half:64 * half + 64, :].rearrange(
                    "p (g h c) -> p g h c", h=2, c=GC)[:, :, half, :], 1.0).then_inc(*cst.mid())
            pool.wait_ge(*cst.mine())

            with pool.Fori(0, DEPTH) as l:
                st = Steps(pool_order, l)
                pool.sem_clear(pool_order)

                def tt(o, i0, i1, op=ALU.mult):
                    return nc.gpsimd.tensor_tensor(o, i0, i1, op)

                def prep(u):
                    pool.wait_ge(*st.at(hi_made, u + 1))
                    c = UW - pool_cols(u)
                    tt(w_lo[u % HL][:, c:], raw[u % RAW][:, c:], f32(w_hi[u % HL][:, c:]), ALU.subtract).then_inc(*st.sig(lo_made_pool))

                cur = [small[:, 16:18, :], small[:, 18:20, :]]

                def power(k):
                    table, n = (pw1 if k < 4 else pw16), 1 << (k % 4)
                    if k == 0:
                        pool.wait_ge(*st.at(cs_ready, 1))
                        tt(cur[0][:, 0, :], COS, ones[:, 0:STILES]).then_inc(*st.mid())
                        tt(cur[0][:, 1, :], SIN, ones[:, 0:STILES]).then_inc(*st.mid())
                        for tb in (pw1, pw16):
                            nc.gpsimd.memset(tb[:, 0, :, 0:1], 1.0).then_inc(*st.mid())
                            nc.gpsimd.memset(tb[:, 1, :, 0:1], 0.0).then_inc(*st.mid())
                        pool.wait_ge(*st.mine())
                    c = cur[k % 2]
                    cr = c[:, 0, :].unsqueeze(2).broadcast_to([P, STILES, n])
                    ci = c[:, 1, :].unsqueeze(2).broadcast_to([P, STILES, n])
                    er, ei = table[:, 0, :, 0:n], table[:, 1, :, 0:n]

                    def part(i):
                        return ptmp[:, 128 * i:128 * i + STILES * n].rearrange("p (s n) -> p s n", n=n)

                    tt(part(0), er, cr).then_inc(*st.mid())
                    tt(part(1), ei, ci).then_inc(*st.mid())
                    tt(part(2), er, ci).then_inc(*st.mid())
                    tt(part(3), ei, cr).then_inc(*st.mid())
                    sq = [small[:, 20 + i, :] for i in range(3)]
                    if k < 7:
                        tt(sq[0], c[:, 0, :], c[:, 0, :]).then_inc(*st.mid())
                        tt(sq[1], c[:, 1, :], c[:, 1, :]).then_inc(*st.mid())
                        tt(sq[2], c[:, 0, :], c[:, 1, :]).then_inc(*st.mid())
                    pool.wait_ge(*st.mine())
                    tt(table[:, 0, :, n:2 * n], part(0), part(1), ALU.subtract).then_inc(*st.mid())
                    tt(table[:, 1, :, n:2 * n], part(2), part(3), ALU.add).then_inc(*st.mid())
                    if k < 7:
                        nxt = cur[(k + 1) % 2]
                        tt(nxt[:, 0, :], sq[0], sq[1], ALU.subtract).then_inc(*st.mid())
                        tt(nxt[:, 1, :], sq[2], sq[2], ALU.add).then_inc(*st.mid())
                    pool.wait_ge(*st.mine())

                def rotations(i):
                    pool.wait_ge(*st.at(rot_used, i - 1))
                    ar, ai = (pw16[:, r, 2 * i:2 * i + 2, :].unsqueeze(3).broadcast_to([P, 2, 16, 16]) for r in (0, 1))
                    br, bi = (pw1[:, r, 2 * i:2 * i + 2, :].unsqueeze(2).broadcast_to([P, 2, 16, 16]) for r in (0, 1))
                    o = [rot[:, i % 2, r, :].rearrange("p (s a b) -> p s a b", a=16, b=16) for r in (0, 1)]
                    pt = ptmp[:, :].rearrange("p (s a b) -> p s a b", a=16, b=16)
                    tt(o[0], ar, br).then_inc(*st.mid())
                    tt(pt, ai, bi).then_inc(*st.mid())
                    pool.wait_ge(*st.mine())
                    tt(o[0], o[0], pt, ALU.subtract).then_inc(*st.mid())
                    tt(o[1], ar, bi).then_inc(*st.mid())
                    pool.wait_ge(*st.mine())
                    tt(pt, ai, br).then_inc(*st.mid())
                    pool.wait_ge(*st.mine())
                    tt(o[1], o[1], pt, ALU.add).then_inc(*st.sig(rot_ready))

                def states_im(i):
                    cs, sn = rot[:, i % 2, 0, :], rot[:, i % 2, 1, :]
                    pool.wait_ge(*st.at(s_used, i))
                    pool.wait_ge(*st.at(v_ready, i + 1))
                    tt(s_re_im[:, 1, :], v_re_im[:, 0, :], sn).then_inc(*st.mid())
                    tt(ptmp[:, :], v_re_im[:, 1, :], cs).then_inc(*st.mid())
                    pool.wait_ge(*st.mine())
                    tt(s_re_im[:, 1, :], s_re_im[:, 1, :], ptmp[:, :], ALU.add).then_inc(*st.sig(s_im_ready))

                def rotate(w):
                    key = ("dq", "dk")[w]
                    pool.wait_ge(*st.at(*freed("T0", (key, 0))))
                    pool.wait_ge(*st.at(*freed("T1", (key, 0))))
                    v = dN[w].rearrange("p t (c d) -> p t c d", d=HD)
                    t1, t2 = v[:, :, :, 0:ROT_HALF], v[:, :, :, ROT_HALF:ROT]
                    cs = [rope[:, i, :, :].unsqueeze(2).broadcast_to([P, NT, 8, ROT_HALF]) for i in (0, 1)]
                    h = [ptmp[:, 128 * i:128 * i + 128].rearrange("p (t c d) -> p t c d", t=NT, c=8) for i in (0, 1)]
                    tt(h[0], t2, cs[1]).then_inc(*st.mid())
                    tt(h[1], t1, cs[1]).then_inc(*st.mid())
                    pool.wait_ge(*st.mine())
                    tt(t1, t1, cs[0]).then_inc(*st.mid())
                    tt(t2, t2, cs[0]).then_inc(*st.mid())
                    pool.wait_ge(*st.mine())
                    tt(t1, t1, h[0], ALU.subtract).then_inc(*st.mid())
                    tt(t2, t2, h[1], ALU.add).then_inc(*st.sig(rope_done))

                for u in range(-1, NU):
                    if u < 0:
                        for n in range(HL):
                            prep(n)
                    elif u + HL < NU:
                        prep(u + HL)
                    for s in SIDE[u]:
                        pool.wait_ge(*st.mine())
                        if s[0] == "ssm_pow":
                            power(s[1])
                        elif s[0] == "ssm_rot0":
                            rotations(0)
                        elif s[0] == "ssm_in" and s[1] + 1 < SSM_STEPS:
                            rotations(s[1] + 1)
                        elif s[0] == "ssm_rot":
                            states_im(s[1])
                        elif s[0] == "rope":
                            rotate(s[1])
                pool.wait_ge(*st.mine())

        @block.scalar
        def _(act):
            def fn(o, i, f=ACT.Copy, **kw):
                return nc.scalar.activation(o, i, f, **kw)

            ast = Steps(pre_act)
            act.dma_start(att[:, 0:512], a["diff_lambda"].rearrange("l k n -> (l k n)").partition_broadcast(P))\
               .then_inc(lam_landed, 16)
            act.dma_start(stat[:, 62:64].bitcast(I32), a["positions"][0].rearrange("(t p) -> p t", p=P),
                          allow_slow_non_contiguous=True).then_inc(pos_landed, 16)
            act.preload_act_table_set("natural_log_exp_and_others")
            act.wait_ge(pre_dve, 1)
            act.wait_ge(mem_landed, 16)
            for t in range(NT):
                fn(memT[:, 4 * t:4 * t + 4, :].rearrange("p k n -> p (k n)"), xn[:, t, :], ACT.Square,
                        accum_out=SS[:, t:t + 1]).then_inc(*ast.mid())
                act.wait_ge(*ast.mine())
            fn(R0, SS, ACT.Ln, scale=1.0 / D, bias=eps[:, 0:1]).then_inc(*ast.mid())
            act.wait_ge(*ast.mine())
            fn(R0, R0, ACT.Exp, scale=-0.5).then_inc(*ast.mid())
            act.wait_ge(*ast.mine())
            act.wait_ge(pre_dve, 4)
            fn(stat[:, 28:32], stat[:, 24:28], ACT.Exp).then_inc(*ast.mid())
            act.wait_ge(*ast.mine())
            act.wait_ge(pre_dve, 6)
            rp = [rope[:, i, :, :].rearrange("p t j -> p (t j)") for i in (0, 1)]
            fn(rp[0], small[:, 5, :], ACT.Abs).then_inc(*ast.mid())
            act.wait_ge(*ast.mine())
            fn(rp[1], small[:, 5, :], ACT.Sin).then_inc(*ast.mid())
            act.wait_ge(*ast.mine())
            fn(rp[0], rp[0], ACT.Sin, scale=-1.0, bias=eps[:, 1:2]).then_inc(*ast.mid())
            act.wait_ge(*ast.mine())

            act.wait_ge(x_landed, 16)

            with act.Fori(0, DEPTH) as l:
                st = Steps(act_order, l)
                act.sem_clear(act_order)

                act.preload_act_table_set("natural_log_exp_and_others")

                def prep(u):
                    act.wait_ge(*st.at(raw_landed[u % RAW], u // RAW + 1))
                    act.wait_ge(*st.at(unit_done, u - HL + 1))
                    fn(w_hi[u % HL][:, :], raw[u % RAW][:, :]).then_inc(*st.sig(hi_made))

                def stats(which, half):
                    for t in range(NT):
                        act.wait_ge(*st.at(*norm_input(which, half, t)))
                        c = slice(512 * half, 512 * half + 512)
                        fn(squares[t], x[:, t, c], ACT.Square, accum_out=(SS1 if half else SS)[:, t:t + 1])\
                            .then_inc(*st.sig(norm_ss))
                    if half == 0 and which == "cross":
                        act.preload_act_table_set("natural_log_exp_and_others")
                    act.wait_ge(*st.mine())
                    if half == 0:
                        fn(SS0V, SS, ACT.Identity, scale=1.0 / D, bias=eps[:, 0:1]).then_inc(*st.mid())
                    else:
                        for t in range(NT):
                            fn(R0[:, t:t + 1], SS1[:, t:t + 1], ACT.Ln, scale=1.0 / D, bias=SS0V[:, t:t + 1])\
                                .then_inc(*st.mid())
                        act.wait_ge(*st.mine())
                        fn(R0, R0, ACT.Exp, scale=-0.5).then_inc(*st.sig(norm_r0))

                def norm(which):
                    if which == "mix":
                        act.wait_ge(*st.at(*freed("T0", ("params",))))
                    g = gain_row[which]
                    for j, b in enumerate(TURN_BANKS):
                        act.wait_ge(*st.at(*freed(b, ("turn_x", which, j // 2))))
                        for k in (2 * j, 2 * j + 1):
                            fn(hT_hi[:, k, :], h_buf[:, k, :], ACT.Identity,
                               scale=col[:, g + k:g + k + 1]).then_inc(*st.sig(norm_hi))

                def ssm_angle():
                    fn(DT, col[:, R_DT:R_DT + 16], ACT.Exp).then_inc(*st.sig(dt_ready))
                    act.wait_ge(*st.at(lam_dt, 1))
                    fn(DECAY, LD, ACT.Exp).then_inc(*st.sig(decay_ready))

                def ssm_cos():
                    act.wait_ge(*st.at(angle_ready, 1))
                    fn(THA, THR, ACT.Abs).then_inc(*st.mid())
                    fn(SIN, THR, ACT.Sin).then_inc(*st.mid())
                    act.wait_ge(*st.mine())
                    fn(COS, THA, ACT.Sin, scale=-1.0, bias=eps[:, 1:2]).then_inc(*st.sig(cs_ready))
                    act.preload_act_table_set("natural_log_exp_and_others")

                def evac(u):
                    key = KEYS[u]
                    if not closes(key):
                        return
                    b = unit_banks(key)
                    kind, use = key[0], (key[0], 0)

                    def take(o, bk, use, f=ACT.Copy, **kw):
                        act.wait_ge(*st.at(unit_done, u + 1))
                        fn(o, bank[bk][:, :], f, **kw).then_inc(*st.sig(*freed(bk, use)))

                    def flat(o):
                        return o.rearrange("p k n -> p (k n)")

                    if kind == "sq":
                        take(flat(qk[:, 2 * key[1]:2 * key[1] + 2, :]), b[0], key, scale=DSCALE)
                    elif kind in ("sv", "xv", "dq", "dk", "dv"):
                        dst = {"sv": vN, "xv": vN, "dq": dN[0], "dk": dN[1], "dv": dv}[kind]
                        for t in range(NT):
                            take(dst[:, t, :], b[t], use)
                    elif isinstance(kind, tuple):
                        n, i = kind[1], key[1]
                        k0 = 2 * i + (8 if n == 2 else 0)
                        dst = gates0[i // 2][:, 2 * (i % 2):2 * (i % 2) + 2, :] if n == 0 else gates[:, k0:k0 + 2, :]
                        take(flat(dst), b[0], key)
                    elif key == ("glu", 1):
                        for j, bk in enumerate(b):
                            take(flat(sg[:, 2 * j:2 * j + 2, :]), bk, key, ACT.Sigmoid)
                    elif key == ("glu", 0):
                        fn(flat(gates[:, 0:8, :]), flat(gates[:, 0:8, :]), ACT.Sigmoid).then_inc(*st.sig(gate_ready))
                        for j, bk in enumerate(b):
                            act.wait_ge(*st.at(*freed(bk, key)))
                            fn(flat(hT_hi[:, 2 * j:2 * j + 2, :]), v_re_im[:, j, :]).then_inc(*st.sig(glu_hi))
                    elif kind == "branch":
                        cb, n = key[1:]
                        if cb == 0 and n == 1:
                            fn(flat(gates[:, 8:16, :]), flat(gates[:, 8:16, :]), ACT.Sigmoid).then_inc(*st.sig(gate_ready))
                        if cb == 0 and n == 2:
                            for g0 in gates0:
                                fn(flat(g0), flat(g0), ACT.Sigmoid).then_inc(*st.sig(gate_ready))
                        if n == 0:
                            for j in range(2):
                                act.wait_ge(*st.at(mg_made, 2 * cb + j + 1))
                                fn(flat(merged(cb)[0][:, 2 * j:2 * j + 2, :]), macc(cb, j)).then_inc(*st.sig(mg_hi))
                    elif kind == "xq":
                        take(flat(qk[:, 2 * key[1]:2 * key[1] + 2, :]), b[0], key)
                    elif kind == "up":
                        g, i = key[1:]
                        if g:
                            act.wait_ge(*st.at(sq_made, 2 * g + i - 1))
                        take(r_b[i], b[0], key, ACT.Relu)
                        act.wait_ge(*st.at(sq_made, 2 * g + i + 1))
                        if g >= 2:
                            act.wait_ge(*st.at(unit_done, AT_UNIT["down", g - 2, 1] + 1))
                        k0 = 4 * (g % 2) + 2 * i
                        fn(flat(bT_hi[:, k0:k0 + 2, :]), q_b[i]).then_inc(*st.sig(hid_hi))

                def stage(s):
                    kind = s[0]
                    if kind == "stats":
                        stats(*s[1:])
                    elif kind == "norm":
                        norm(s[1])
                    elif kind == "ssm_angle":
                        ssm_angle()
                    elif kind == "ssm_f":
                        ssm_cos()
                    elif kind == "turn":
                        for j, b in enumerate(("X0", "X1")):
                            act.wait_ge(*st.at(*full_at(b, s)))
                            k0 = 4 * s[1] + 2 * j
                            fn(dT[:, k0:k0 + 2, :].rearrange("p k n -> p (k n)"), bank[b][:, :])\
                                .then_inc(*st.sig(*freed(b, s)))
                    elif kind == "sb_u":
                        z = z_b[s[1] % 2]
                        act.wait_ge(*st.at(*freed("X1", s)))
                        fn(z, z, ACT.Exp).then_inc(*st.sig(w_ready))
                    elif kind == "sb_p" and s[1] % 2:
                        act.wait_ge(*st.at(sbp_done, s[1] + 1))
                        fn(bT_hi[:, 4 + s[1] // 2, :], bank["A3"][:, 0:T]).then_inc(*st.sig(sb_hi))
                    elif kind == "da_t":
                        j = s[1]
                        nk = P * (j // DA_HEADS + 1)
                        act.wait_ge(*st.at(*full_at("X1", s)))
                        if j >= 2:
                            act.wait_ge(*st.at(dap_done, j - 1))
                        fn(pT_b[j % 2][:, 0:nk], bank["X1"][:, 0:nk]).then_inc(*st.sig(*freed("X1", s)))
                    elif kind == "da_o":
                        qt = s[1]
                        act.wait_ge(*st.at(*full_at("X1", s)))
                        fn(bT_hi[:, 8:12, qt * P:qt * P + P], bank["X1"][:, :].rearrange("p (h n) -> p h n", n=P),
                                  ACT.Identity, scale=GSUB).then_inc(*st.sig(da_hi))
                    elif kind == "memg":
                        act.wait_ge(*st.at(unit_done, AT_UNIT["branch", 1, 0] + 1))
                        for k in range(KD):
                            fn(bT_hi[:, 4 + k, :], memT[:, k, :], ACT.Identity,
                                      scale=col[:, R_MEM + k:R_MEM + k + 1]).then_inc(*st.sig(mem_hi))
                    elif kind == "xa_s":
                        h = s[1]
                        b = stage_banks(s)[0]
                        act.wait_ge(*st.at(xmax_ready, h + 1))
                        for qt in range(NT):
                            ins = fn(e_b[h][:, qt, :], bank[b][:, qt * T:qt * T + T], ACT.Exp, scale=XSCALE,
                                     bias=XNB[h][:, qt:qt + 1], accum_out=XRS[h][:, qt:qt + 1])
                            ins.then_inc(*st.sig(*freed(b, s))) if qt else ins.then_inc(*st.mid())
                    elif kind == "xa_t":
                        h = s[1]
                        b = stage_banks(s)[0]
                        act.wait_ge(*st.at(*full_at(b, s)))
                        fn(eT_b[h].rearrange("p m n -> p (m n)"), bank[b][:, :]).then_inc(*st.sig(*freed(b, s)))
                    elif kind == "xa_p":
                        h = s[1]
                        b = stage_banks(s)[0]
                        act.wait_ge(*st.at(*full_at(b, s)))
                        fn(bT_hi[:, h, :], bank[b][:, 0:T]).then_inc(*st.sig(xo_hi))

                def later(s):
                    kind = s[0]
                    if kind == "sb_s":
                        z, nl = z_b[s[1] % 2], nl_b[s[1] % 2]
                        act.wait_ge(*st.at(*freed("X0", s)))
                        fn(nl, z, ACT.Abs).then_inc(*st.mid())
                        act.wait_ge(*st.mine())
                        fn(nl, nl, ACT.Exp, scale=-1.0).then_inc(*st.mid())
                        act.wait_ge(*st.mine())
                        fn(nl, nl, ACT.Ln, bias=1.0).then_inc(*st.sig(ln_ready))
                    elif kind == "da_s":
                        j = s[1]
                        nk = P * (j // DA_HEADS + 1)
                        act.wait_ge(*st.at(dmax_ready, j + 1))
                        for c in range(2):
                            ins = fn(p_b[j % 2][:, c, 0:nk], p_b[j % 2][:, c, 0:nk], ACT.Exp, scale=DSCALE,
                                     bias=DNB[j % 2][:, c:c + 1], accum_out=DRS[j % 2][:, c:c + 1])
                            ins.then_inc(*st.sig(dexp_ready)) if c else ins.then_inc(*st.mid())
                    elif kind == "da_n":
                        qt = s[1]
                        act.wait_ge(*st.at(oss_ready, qt + 1))
                        fn(OR0, OSS, ACT.Ln, scale=1.0 / P, bias=eps[:, 0:1]).then_inc(*st.mid())
                        act.wait_ge(*st.mine())
                        fn(OR0, OR0, ACT.Exp, scale=-0.5).then_inc(*st.sig(o_r0))
                    elif kind == "gelu":
                        act.wait_ge(*st.at(*freed("A2", ("ssm_out", SSM_STEPS - 2))))
                        gl = v_re_im[:, :, :].rearrange("p r (k n) -> p (r k) n", n=T)
                        for k in range(KB):
                            fn(gl[:, k, :], uT[:, k, :], ACT.Gelu_apprx_tanh).then_inc(*st.mid())
                        act.wait_ge(*st.mine())
                        for k in range(KB):
                            fn(bT_hi[:, k, :], gl[:, k, :]).then_inc(*st.sig(gelu_hi))
                        act.preload_act_table_set("natural_log_exp_and_others")

                for u in range(-1, NU):
                    nxt = list(range(HL)) if u < 0 else [u + HL] if u + HL < NU else []
                    if u >= 0 and u not in PREP_BEFORE_EVAC:
                        evac(u)
                    n_first = len(nxt) if u in ACT_PREP_EARLY else 0
                    for n in nxt[:n_first]:
                        prep(n)
                    if u in PREP_BEFORE_EVAC:
                        evac(u)
                    for s in SIDE[u]:
                        if s == ("norm", "mix"):
                            prep(nxt[0])
                            n_first = 1
                        if st.last:
                            act.wait_ge(*st.mine())
                        stage(s)
                    for n in nxt[n_first:]:
                        prep(n)
                    for s in SIDE[u]:
                        act.wait_ge(*st.mine())
                        later(s)
                act.wait_ge(*st.mine())
            for half in range(2):
                for t in range(NT):
                    b = f"A{2 * half + t}"
                    act.wait_ge(free[b].sem, free[b].value(DEPTH, 0))
                    if half:
                        act.wait_ge(end_act, 1 + t)
                    c = slice(512 * half, 512 * half + 512)
                    fn(squares[t], x[:, t, c], ACT.Square, accum_out=(SS1 if half else SS)[:, t:t + 1])\
                        .then_inc(end_act, 1)
            act.wait_ge(end_act, 4)
            fn(SS0V, SS, ACT.Identity, scale=1.0 / D, bias=eps[:, 0:1]).then_inc(end_act, 1)
            act.wait_ge(end_act, 5)
            for t in range(NT):
                fn(R0[:, t:t + 1], SS1[:, t:t + 1], ACT.Ln, scale=1.0 / D, bias=SS0V[:, t:t + 1]).then_inc(end_act, 1)
            act.wait_ge(end_act, 7)
            fn(R0, R0, ACT.Exp, scale=-0.5).then_inc(end_act, 1)

        @block.vector
        def _(dve):
            V = nc.vector

            def newton(c, r0, ss, n, v, t, r):
                V.tensor_scalar(v, ss, 1.0 / n, RMS_EPS, ALU.mult, ALU.add).then_inc(*c.mid())
                V.tensor_tensor(t, r0, r0, ALU.mult).then_inc(*c.mid())
                dve.wait_ge(*c.mine())
                V.tensor_tensor(t, t, v, ALU.mult).then_inc(*c.mid())
                dve.wait_ge(*c.mine())
                V.tensor_scalar(t, t, -0.5, 1.5, ALU.mult, ALU.add).then_inc(*c.mid())
                dve.wait_ge(*c.mine())
                V.tensor_tensor(r, r0, t, ALU.mult).then_inc(*c.mid())
                dve.wait_ge(*c.mine())

            def reduce_angle(c, th, k, o):
                V.tensor_scalar(k, th, 1.0 / TWO_PI, ROUND, ALU.mult, ALU.add).then_inc(*c.mid())
                dve.wait_ge(*c.mine())
                V.tensor_scalar(k, k, ROUND, None, ALU.subtract).then_inc(*c.mid())
                dve.wait_ge(*c.mine())
                V.scalar_tensor_tensor(out=o, in0=k, scalar=-PI_HI, in1=th, op0=ALU.mult, op1=ALU.add)\
                 .then_inc(*c.mid())
                dve.wait_ge(*c.mine())
                V.scalar_tensor_tensor(out=o, in0=k, scalar=-PI_MID, in1=o, op0=ALU.mult, op1=ALU.add)\
                 .then_inc(*c.mid())
                dve.wait_ge(*c.mine())
                V.scalar_tensor_tensor(out=o, in0=k, scalar=-PI_LO, in1=o, op0=ALU.mult, op1=ALU.add)\
                 .then_inc(*c.mid())
                dve.wait_ge(*c.mine())

            pst, mst = Steps(dve_order), Steps(pre_dve)

            V.memset(eps[:, 0:1], RMS_EPS).then_inc(*pst.mid())
            V.memset(eps[:, 1:2], math.pi / 2).then_inc(*pst.mid())
            V.memset(small[:, :, :], 0.0).then_inc(*pst.mark(mst))
            dve.wait_ge(*pst.mine())
            dve.wait_ge(consts_made, 12)
            dve.wait_ge(pre_act, 4)
            newton(pst, R0, SS, D, VV, TT, RSTD)
            for t in range(NT):
                V.tensor_scalar(dg[t], ident[:, :], RSTD[:, t:t + 1], None, ALU.mult).then_inc(*pst.mark(mst))
            dve.wait_ge(lam_landed, 16)
            lv = att[:, 0:512].rearrange("p (m b n) -> p m b n", b=2, n=HD)
            pr = att[:, 512:768].rearrange("p (m n) -> p m n", n=HD)
            V.tensor_tensor(pr, lv[:, :, 0, :], lv[:, :, 1, :], ALU.mult).then_inc(*pst.mid())
            dve.wait_ge(*pst.mine())
            V.tensor_reduce(stat[:, 24:28], pr, AX.X, ALU.add).then_inc(*pst.mark(mst))
            dve.wait_ge(pos_landed, 16)
            V.tensor_copy(stat[:, 10:12], stat[:, 62:64].bitcast(I32)).then_inc(*pst.mid())
            dve.wait_ge(*pst.mine())
            inv = (np.float32(ROPE_THETA) ** (-np.arange(0, ROT, 2, dtype=np.float32) / np.float32(ROT))).astype(np.float32)
            ang = small[:, 4, :].rearrange("p (t j) -> p t j", t=NT)
            for j in range(ROT_HALF):
                V.tensor_scalar(ang[:, :, j], stat[:, 10:12], float(inv[j]), None, ALU.mult).then_inc(*pst.mid())
            dve.wait_ge(*pst.mine())
            V.tensor_copy(small[:, 3, :], small[:, 4, :]).then_inc(*pst.mark(mst))
            dve.wait_ge(*pst.mine())
            reduce_angle(pst, small[:, 3, :], small[:, 4, :], small[:, 5, :])
            V.tensor_scalar(small[:, 5, :], small[:, 5, :], PI_SAFE, -PI_SAFE, ALU.min, ALU.max).then_inc(*pst.mark(mst))
            dve.wait_ge(pre_act, 5)
            for i in range(DEPTH):
                init = 0.8 - 0.6 * math.exp(-0.3 * i)
                e0, e1 = stat[:, 28 + 2 * i:29 + 2 * i], stat[:, 29 + 2 * i:30 + 2 * i]
                V.tensor_tensor(lam_all[:, 0, i:i + 1], e1, e0, ALU.subtract).then_inc(*pst.mid())
                dve.wait_ge(*pst.mine())
                V.tensor_scalar(lam_all[:, 0, i:i + 1], lam_all[:, 0, i:i + 1], init, None, ALU.subtract).then_inc(*pst.mid())
                V.memset(lam_all[:, 1, i:i + 1], 1.0 - init).then_inc(*pst.mid())
            dve.wait_ge(pre_pe, 1)
            V.tensor_copy(gmask[:, :], bank["A0"][:, 0:P]).then_inc(*pst.mark(mst))
            for j, b in enumerate(TURN_BANKS):
                dve.wait_ge(pre_pe, 2 + j)
                V.tensor_copy(memT[:, 2 * j:2 * j + 2, :].rearrange("p k n -> p (k n)"), bank[b][:, :]).then_inc(*pst.mark(mst))
            dve.wait_ge(*pst.mine())
            dve.wait_ge(x_landed, 16)

            with dve.Fori(0, DEPTH) as l:
                st = Steps(dve_order, l)
                dve.sem_clear(dve_order)

                def tt(o, i0, i1, op=ALU.mult):
                    return V.tensor_tensor(o, i0, i1, op)

                def flat(o):
                    return o.rearrange("p k n -> p (k n)")

                def prep(u):
                    dve.wait_ge(*st.at(hi_made, u + 1))
                    c = UW - pool_cols(u)
                    tt(w_lo[u % HL][:, 0:c], raw[u % RAW][:, 0:c], f32(w_hi[u % HL][:, 0:c]), ALU.subtract).then_inc(*st.sig(lo_made))

                def spread():
                    dve.wait_ge(*st.at(prm_landed, 9))
                    V.tensor_copy(prm[R_DT:R_DT + 16, :].rearrange("p (g s) -> p g s", g=2),
                                         ldt[R_DT:R_DT + 16, :].unsqueeze(2).broadcast_to([16, 2, STATES])).then_inc(*st.sig(prm_spread))

                def params():
                    dve.wait_ge(*st.at(*full_at("T0", ("params",))))
                    V.tensor_copy(col[:, :], bank["T0"][:, 0:R_END]).then_inc(*st.sig(*freed("T0", ("params",))))
                    dve.wait_ge(*st.mine())
                    V.tensor_copy(lam[:, :], lam_all[:, :, bass.ds(l, 1)].rearrange("p a b -> p (a b)")).then_inc(*st.mid())
                    dve.wait_ge(*st.mine())
                    tt(GSUB, col[:, R_SUBLN:R_SUBLN + 1], lam[:, 1:2]).then_inc(*st.sig(prm_read))

                def stats(which):
                    n = NORMS.index(which)
                    dve.wait_ge(*st.at(norm_ss, 2 * NT * (n + 1)))
                    V.scalar_tensor_tensor(out=VV, in0=SS1, scalar=1.0 / D, in1=SS0V, op0=ALU.mult, op1=ALU.add)\
                     .then_inc(*st.mid())
                    dve.wait_ge(*st.mine())
                    dve.wait_ge(*st.at(norm_r0, n + 1))
                    for t in range(NT):
                        V.scalar_tensor_tensor(out=TT[:, t:t + 1], in0=R0[:, t:t + 1], scalar=R0[:, t:t + 1],
                                               in1=VV[:, t:t + 1], op0=ALU.mult, op1=ALU.mult).then_inc(*st.mid())
                    dve.wait_ge(*st.mine())
                    V.tensor_scalar(TT, TT, -0.5, 1.5, ALU.mult, ALU.add).then_inc(*st.mid())
                    dve.wait_ge(*st.mine())
                    for t in range(NT):
                        V.tensor_scalar(dg[t], ident[:, :], R0[:, t:t + 1], TT[:, t:t + 1], ALU.mult, ALU.mult)\
                         .then_inc(*st.sig(diag_ready))

                def norm(which):
                    n = NORMS.index(which)
                    g = gain_row[which]
                    dve.wait_ge(*st.at(*full_at("A1", ("norm", which))))
                    V.tensor_copy(r_row, bank["A1"][:, 0:T]).then_inc(*st.sig(*freed("A1", ("norm", which))))
                    dve.wait_ge(*st.mine())
                    for j in range(KD // 2 + 1):
                        if j < KD // 2:
                            b, turned = TURN_BANKS[j], ("turn_x", which, j // 2)
                            dve.wait_ge(*st.at(*full_at(b, turned)))
                            tt(h_buf[:, 2 * j:2 * j + 2, :], bank[b][:, :].rearrange("p (k n) -> p k n", k=2),
                               r_row.unsqueeze(1).broadcast_to([P, 2, T])).then_inc(*st.sig(*freed(b, turned)))
                        if j:
                            dve.wait_ge(*st.at(norm_hi, KD * n + 2 * j))
                            for k in (2 * j - 2, 2 * j - 1):
                                ins = V.scalar_tensor_tensor(
                                    out=hT_lo[:, k, :], in0=h_buf[:, k, :], scalar=col[:, g + k:g + k + 1],
                                    in1=f32(hT_hi[:, k, :]), op0=ALU.mult, op1=ALU.subtract)
                                ins.then_inc(*st.sig(h_ready)) if k % 2 else ins.then_inc(*st.mid())

                def ssm_angle():
                    lre, lim = col[:, R_LRE:R_LRE + 16], col[:, R_LIM:R_LIM + 16]
                    dve.wait_ge(*st.at(dt_ready, 1))
                    tt(LD, lre, DT).then_inc(*st.mid())
                    tt(TH, lim, DT).then_inc(*st.sig(lam_dt))
                    dve.wait_ge(*st.mine())
                    reduce_angle(st, TH, KK, THR)
                    V.tensor_scalar(THR, THR, PI_SAFE, -PI_SAFE, ALU.min, ALU.max).then_inc(*st.sig(angle_ready))

                def ssm_f():
                    lre, lim = col[:, R_LRE:R_LRE + 16], col[:, R_LIM:R_LIM + 16]
                    dve.wait_ge(*st.at(cs_ready, 1))
                    tt(LBR, DECAY, COS).then_inc(*st.mid())
                    tt(LBI, DECAY, SIN).then_inc(*st.mid())
                    tt(T1, lre, lre).then_inc(*st.mid())
                    tt(T2, lim, lim).then_inc(*st.mid())
                    dve.wait_ge(*st.mine())
                    V.tensor_scalar(LBR, LBR, -1.0, None, ALU.add).then_inc(*st.mid())
                    tt(DEN, T1, T2, ALU.add).then_inc(*st.mid())
                    dve.wait_ge(*st.mine())
                    V.reciprocal(DEN, DEN).then_inc(*st.mid())
                    tt(T1, LBR, lre).then_inc(*st.mid())
                    tt(T2, LBI, lim).then_inc(*st.mid())
                    dve.wait_ge(*st.mine())
                    tt(FR, T1, T2, ALU.add).then_inc(*st.mid())
                    dve.wait_ge(*st.mine())
                    tt(T1, LBI, lre).then_inc(*st.mid())
                    tt(T2, LBR, lim).then_inc(*st.mid())
                    dve.wait_ge(*st.mine())
                    tt(FI, T1, T2, ALU.subtract).then_inc(*st.mid())
                    dve.wait_ge(*st.mine())
                    tt(FR, FR, DEN).then_inc(*st.mid())
                    tt(FI, FI, DEN).then_inc(*st.mid())

                def ssm_b():
                    dve.wait_ge(*st.at(mat_landed, 6))
                    dve.wait_ge(*st.mine())

                    def bb(i):
                        return b_raw[:, i, :].rearrange("p (i c) -> p i c", c=GC)

                    def prod(i):
                        return tmp[:, i, 0:256].rearrange("p (i c) -> p i c", c=GC)

                    def dup(t3):
                        return t3.unsqueeze(2).broadcast_to([P, STILES, 2, GC])

                    fr, fi = (f.unsqueeze(2).broadcast_to([P, STILES, GC]) for f in (FR, FI))
                    for r, (f0, f1, op) in enumerate(((fr, fi, ALU.subtract), (fi, fr, ALU.add))):
                        tt(prod(0), bb(0), f0).then_inc(*st.mid())
                        tt(prod(1), bb(1), f1).then_inc(*st.mid())
                        dve.wait_ge(*st.mine())
                        ins = tt(bN[:, r, :].rearrange("p (i h c) -> p i h c", h=2, c=GC), dup(prod(0)), dup(prod(1)), op)
                        ins.then_inc(*st.sig(b_ready)) if r else ins.then_inc(*st.mid())
                        dve.wait_ge(*st.mine())

                def ssm_bt():
                    for r, b in enumerate(("A0", "A1")):
                        dve.wait_ge(*st.at(*full_at(b, ("ssm_bt",))))
                        tt(bt[:, r, :, :], bank[b][:, :].rearrange("p (k n) -> p k n", n=P),
                                  gmask[:, :].unsqueeze(1).broadcast_to([P, 4, P])).then_inc(*st.sig(*freed(b, ("ssm_bt",))))

                def ssm_ct():
                    for r, b in enumerate(("A2", "A3")):
                        dve.wait_ge(*st.at(*full_at(b, ("ssm_ct",))))
                        for k in range(4):
                            ins = V.scalar_tensor_tensor(out=ct[:, r, k, :], in0=bank[b][:, k * P:k * P + P],
                                                         scalar=(-1.0 if r else 1.0), in1=gmaskT[:, :],
                                                         op0=ALU.mult, op1=ALU.mult)
                            ins.then_inc(*st.sig(*freed(b, ("ssm_ct",)))) if k == 3 else ins.then_inc(*st.mid())

                def ssm_in(i):
                    s = ("ssm_in", i)
                    cs, sn = rot[:, i % 2, 0, :], rot[:, i % 2, 1, :]
                    dve.wait_ge(*st.at(rot_ready, i + 1))
                    if i:
                        dve.wait_ge(*st.at(s_im_ready, i))
                    for j, b in enumerate(("A0", "A1")):
                        c = slice(j * T, j * T + T)
                        io = bank[b][:, :].rearrange("p (r n) -> p r n", r=2)
                        dve.wait_ge(*st.at(*full_at(b, s)))
                        tt(v_re_im[:, :, c], io, cs[:, c].unsqueeze(1).broadcast_to([P, 2, T])).then_inc(*st.mid())
                        tt(tmp[:, :, c], io, sn[:, c].unsqueeze(1).broadcast_to([P, 2, T])).then_inc(*st.sig(*freed(b, s)))
                    dve.wait_ge(*st.mine())
                    tt(v_re_im[:, 0, :], v_re_im[:, 0, :], tmp[:, 1, :], ALU.add).then_inc(*st.mid())
                    tt(v_re_im[:, 1, :], v_re_im[:, 1, :], tmp[:, 0, :], ALU.subtract).then_inc(*st.mid())
                    dve.wait_ge(*st.mine())
                    for r in range(2):
                        for j in range(2):
                            vt = v_re_im[:, r, j * T:j * T + T]
                            ins = V.tensor_tensor_scan(vt, DECAY[:, 2 * i + j:2 * i + j + 1].broadcast_to([P, T]),
                                                       vt, 0.0, ALU.mult, ALU.add)
                            ins.then_inc(*st.sig(v_ready)) if r and j else ins.then_inc(*st.mid())

                def ssm_rot(i):
                    cs, sn = rot[:, i % 2, 0, :], rot[:, i % 2, 1, :]
                    dve.wait_ge(*st.at(s_used, i))
                    dve.wait_ge(*st.mine())
                    tt(s_re_im[:, 0, :], v_re_im[:, 0, :], cs).then_inc(*st.mid())
                    tt(tmp[:, 0, :], v_re_im[:, 1, :], sn).then_inc(*st.sig(rot_used))
                    dve.wait_ge(*st.mine())
                    tt(s_re_im[:, 0, :], s_re_im[:, 0, :], tmp[:, 0, :], ALU.subtract).then_inc(*st.sig(s_ready))

                def residual(key, banks):
                    dve.wait_ge(*st.at(unit_done, AT_UNIT[key] + 1))
                    for t, b in enumerate(banks):
                        use = ("down",) if key[0] == "down" else ("wout", key[1] - 1) if key[0] == "wout" else key
                        tt(x_part(t, key), x_part(t, key), bank[b][:, :], ALU.add).then_inc(*st.sig(*freed(b, use)))

                def evac(u):
                    key = KEYS[u]
                    if not closes(key):
                        return
                    b = unit_banks(key)
                    kind, use = key[0], (key[0], 0)

                    def take(o, bk, use):
                        dve.wait_ge(*st.at(unit_done, u + 1))
                        V.tensor_copy(o, bank[bk][:, :]).then_inc(*st.sig(*freed(bk, use)))

                    if kind == "u":
                        take(flat(uT[:, 2 * key[1]:2 * key[1] + 2, :]), b[0], key)
                    elif kind in ("sk", "xk"):
                        take(flat(qk[:, 4 + 2 * key[1]:6 + 2 * key[1], :]), b[0], key)
                    elif key == ("glu", 0):
                        dve.wait_ge(*st.at(unit_done, u + 1))
                        for j, bk in enumerate(b):
                            dve.wait_ge(*st.at(*freed(["T0", "T1"][j], ("glu", 1))))
                            tt(v_re_im[:, j, :], bank[bk][:, :], flat(sg[:, 2 * j:2 * j + 2, :])).then_inc(*st.sig(*freed(bk, key)))
                        for j in range(2):
                            dve.wait_ge(*st.at(glu_hi, j + 1))
                            tt(flat(hT_lo[:, 2 * j:2 * j + 2, :]), v_re_im[:, j, :],
                                      f32(flat(hT_hi[:, 2 * j:2 * j + 2, :])), ALU.subtract).then_inc(*st.sig(glu_ready))
                    elif kind == "branch":
                        cb, n = key[1:]
                        dve.wait_ge(*st.at(unit_done, u + 1))
                        dve.wait_ge(*st.at(gate_ready, {1: 1, 2: 2, 0: 3 + cb}[n]))
                        for j, bk in enumerate(b):
                            k0 = 4 * cb + 2 * j + (8 if n == 2 else 0)
                            g = flat(gates0[cb][:, 2 * j:2 * j + 2, :] if n == 0 else gates[:, k0:k0 + 2, :])
                            if n == 1:
                                tt(macc(cb, j), bank[bk][:, :], g).then_inc(*st.sig(*freed(bk, key)))
                                continue
                            tt(tmp[:, j, :], bank[bk][:, :], g).then_inc(*st.sig(*freed(bk, key)))
                        if n != 1:
                            dve.wait_ge(*st.mine())
                            for j in range(2):
                                ins = tt(macc(cb, j), macc(cb, j), tmp[:, j, :], ALU.add)
                                ins.then_inc(*st.sig(mg_made)) if n == 0 else ins.then_inc(*st.mid())
                            dve.wait_ge(*st.mine())
                        if n == 0:
                            for j in range(2):
                                dve.wait_ge(*st.at(mg_hi, 2 * cb + j + 1))
                                hi, lo = merged(cb)
                                tt(flat(lo[:, 2 * j:2 * j + 2, :]), macc(cb, j),
                                          f32(flat(hi[:, 2 * j:2 * j + 2, :])), ALU.subtract).then_inc(*st.sig(mg_ready))
                    elif kind in ("wout", "xo", "down"):
                        residual(key, b)
                    elif kind == "up":
                        g, i = key[1:]
                        dve.wait_ge(*st.at(*freed(b[0], key)))
                        tt(q_b[i], r_b[i], r_b[i]).then_inc(*st.sig(sq_made))
                        dve.wait_ge(*st.at(hid_hi, 2 * g + i + 1))
                        k0 = 4 * (g % 2) + 2 * i
                        tt(flat(bT_lo[:, k0:k0 + 2, :]), q_b[i], f32(flat(bT_hi[:, k0:k0 + 2, :])),
                                  ALU.subtract).then_inc(*st.sig(hid_ready))

                def stage(s):
                    kind = s[0]
                    if kind == "spread":
                        spread()
                    elif kind == "params":
                        params()
                    elif kind == "stats" and s[2]:
                        stats(s[1])
                    elif kind == "norm":
                        norm(s[1])
                    elif kind == "ssm_angle":
                        ssm_angle()
                    elif kind == "ssm_f":
                        ssm_f()
                    elif kind == "ssm_b":
                        ssm_b()
                    elif kind == "ssm_bt":
                        ssm_bt()
                    elif kind == "ssm_ct":
                        ssm_ct()
                    elif kind == "sb_s":
                        h = s[1]
                        if h >= 2:
                            dve.wait_ge(*st.at(sbp_done, h - 1))
                        dve.wait_ge(*st.at(*full_at("X0", s)))
                        z = z_b[h % 2]
                        tt(z[:, 0:T], bank["X0"][:, 0:T], mask_s, ALU.min).then_inc(*st.mid())
                        tt(z[:, T:384], bank["X0"][:, T:384], mask_s[:, 0:P], ALU.min).then_inc(*st.sig(*freed("X0", s)))
                    elif kind == "sb_u":
                        z = z_b[s[1] % 2]
                        dve.wait_ge(*st.at(*full_at("X1", s)))
                        tt(z, z, bank["X1"][:, 0:384], ALU.subtract).then_inc(*st.sig(*freed("X1", s)))
                    elif kind == "sb_p" and s[1] % 2:
                        k = s[1] // 2
                        dve.wait_ge(*st.at(sb_hi, k + 1))
                        tt(bT_lo[:, 4 + k, :], bank["A3"][:, 0:T], f32(bT_hi[:, 4 + k, :]), ALU.subtract).then_inc(*st.sig(*freed("A3", ("sb_p", s[1] - 1))))
                    elif kind == "da_s":
                        j = s[1]
                        qt = j // DA_HEADS
                        nk = P * (qt + 1)
                        p = p_b[j % 2][:, :, 0:nk]
                        if j >= 2:
                            dve.wait_ge(*st.at(*full_at("X1", ("da_t", j - 2))))
                        for c, b in enumerate(("X0", "X1")):
                            dve.wait_ge(*st.at(*full_at(b, s)))
                            tt(p[:, c, :], bank[b][:, 0:nk], mask_n[:, T - nk:T], ALU.min).then_inc(*st.sig(*freed(b, s)))
                        dve.wait_ge(*st.mine())
                        V.tensor_reduce(DMX, p, AX.X, ALU.max).then_inc(*st.mid())
                        dve.wait_ge(*st.mine())
                        V.tensor_scalar(DNB[j % 2], DMX, -DSCALE, None, ALU.mult).then_inc(*st.sig(dmax_ready))
                    elif kind == "da_n":
                        qt = s[1]
                        dve.wait_ge(*st.at(dap_done, DA_HEADS * (qt + 1)))
                        V.tensor_copy(o_b, bank["A3"][:, :]).then_inc(*st.sig(*freed("A3", ("da_p", DA_HEADS * qt))))
                    elif kind == "da_o":
                        qt = s[1]
                        dve.wait_ge(*st.at(da_hi, qt + 1))
                        V.scalar_tensor_tensor(
                            out=bT_lo[:, 8:12, qt * P:qt * P + P], in0=bank["X1"][:, :].rearrange("p (h n) -> p h n", n=P),
                            scalar=GSUB, in1=f32(bT_hi[:, 8:12, qt * P:qt * P + P]), op0=ALU.mult, op1=ALU.subtract).then_inc(*st.sig(*freed("X1", s)))
                    elif kind == "memg":
                        for k in range(KD):
                            dve.wait_ge(*st.at(mem_hi, k + 1))
                            V.scalar_tensor_tensor(out=bT_lo[:, 4 + k, :], in0=memT[:, k, :],
                                                          scalar=col[:, R_MEM + k:R_MEM + k + 1],
                                                          in1=f32(bT_hi[:, 4 + k, :]), op0=ALU.mult, op1=ALU.subtract).then_inc(*st.sig(mem_ready))
                    elif kind == "xa_s":
                        h = s[1]
                        b = stage_banks(s)[0]
                        dve.wait_ge(*st.at(*full_at(b, s)))
                        V.tensor_reduce(DMX, bank[b][:, :].rearrange("p (t n) -> p t n", t=NT), AX.X, ALU.max).then_inc(*st.mid())
                        dve.wait_ge(*st.mine())
                        V.tensor_scalar(XNB[h], DMX, -XSCALE, None, ALU.mult).then_inc(*st.sig(xmax_ready))
                        dve.wait_ge(*st.mine())
                    elif kind == "xa_w":
                        h = s[1]
                        dve.wait_ge(*st.at(*freed(stage_banks(("xa_s", h))[0], ("xa_s", h))))
                        V.reciprocal(DRR, XRS[h]).then_inc(*st.mid())
                        dve.wait_ge(*st.mine())
                        tt(e_b[h], e_b[h], DRR.unsqueeze(2).broadcast_to([P, NT, T])).then_inc(*st.sig(xw_ready))
                        dve.wait_ge(*st.mine())
                    elif kind == "xa_p":
                        h = s[1]
                        b = stage_banks(s)[0]
                        dve.wait_ge(*st.at(xo_hi, h + 1))
                        tt(bT_lo[:, h, :], bank[b][:, 0:T], f32(bT_hi[:, h, :]), ALU.subtract).then_inc(*st.sig(*freed(b, s)))

                def later(s):
                    kind = s[0]
                    if kind == "sb_s":
                        z, nl = z_b[s[1] % 2], nl_b[s[1] % 2]
                        dve.wait_ge(*st.at(ln_ready, s[1] + 1))
                        V.scalar_tensor_tensor(out=nl, in0=z, scalar=0.0, in1=nl, op0=ALU.max, op1=ALU.add)\
                         .then_inc(*st.sig(nl_ready))
                    elif kind == "da_s":
                        j = s[1]
                        nk = P * (j // DA_HEADS + 1)
                        p = p_b[j % 2]
                        dve.wait_ge(*st.at(dexp_ready, j + 1))
                        V.reciprocal(DRR, DRS[j % 2]).then_inc(*st.mid())
                        dve.wait_ge(*st.mine())
                        tt(DR2, DRR[:, 1:2], lam[:, 0:1]).then_inc(*st.mid())
                        V.tensor_scalar(p[:, 0, 0:nk], p[:, 0, 0:nk], DRR[:, 0:1], None, ALU.mult).then_inc(*st.mid())
                        dve.wait_ge(*st.mine())
                        V.scalar_tensor_tensor(out=p[:, 0, 0:nk], in0=p[:, 1, 0:nk], scalar=DR2,
                                                      in1=p[:, 0, 0:nk], op0=ALU.mult, op1=ALU.add).then_inc(*st.sig(dw_ready))
                    elif kind == "ssm_in":
                        ssm_in(s[1])
                    elif kind == "ssm_rot":
                        ssm_rot(s[1])
                    elif kind == "ssm_out" and s[1] % 2:
                        k = s[1] // 2
                        dve.wait_ge(*st.at(s_used, s[1] + 1))
                        V.scalar_tensor_tensor(out=uT[:, k, :], in0=uT[:, k, :], scalar=col[:, R_D + k:R_D + k + 1],
                                                      in1=bank["A2"][:, 0:T], op0=ALU.mult, op1=ALU.add).then_inc(*st.sig(*freed("A2", ("ssm_out", s[1] - 1))))
                    elif kind == "da_n":
                        qt = s[1]
                        o4 = o_b.rearrange("p (h n) -> p h n", n=P)
                        sq4 = att[:, 0:512].rearrange("p (h n) -> p h n", n=P)
                        tt(sq4, o4, o4).then_inc(*st.mid())
                        dve.wait_ge(*st.mine())
                        V.tensor_reduce(OSS, sq4, AX.X, ALU.add).then_inc(*st.sig(oss_ready))
                        dve.wait_ge(*st.at(o_r0, qt + 1))
                        newton(st, OR0, OSS, P, OVV, OTT, ORSTD)
                        tt(o4, o4, ORSTD.unsqueeze(2).broadcast_to([P, 4, P])).then_inc(*st.sig(on_ready))
                    elif kind == "gelu":
                        gl = v_re_im[:, :, :].rearrange("p r (k n) -> p (r k) n", n=T)
                        for k in range(KB):
                            dve.wait_ge(*st.at(gelu_hi, k + 1))
                            tt(bT_lo[:, k, :], gl[:, k, :], f32(bT_hi[:, k, :]), ALU.subtract).then_inc(*st.sig(gelu_ready))

                for u in range(-1, NU):
                    nxt = list(range(HL)) if u < 0 else [u + HL] if u + HL < NU else []
                    if u >= 0 and u not in PREP_BEFORE_EVAC:
                        evac(u)
                    n_first = len(nxt) if u in DVE_PREP_EARLY else 0
                    for n in nxt[:n_first]:
                        prep(n)
                    if u in PREP_BEFORE_EVAC:
                        evac(u)
                    for s in SIDE[u]:
                        if s == ("norm", "mix"):
                            prep(nxt[0])
                            n_first = 1
                        if st.last:
                            dve.wait_ge(*st.mine())
                        stage(s)
                    for n in nxt[n_first:]:
                        prep(n)
                    for s in SIDE[u]:
                        dve.wait_ge(*st.mine())
                        later(s)
                dve.wait_ge(*st.mine())
            est = Steps(end_dve)
            dve.wait_ge(nf_landed, 16)
            for t in range(NT):
                V.tensor_tensor(xn[:, t, :], x[:, t, :], uT[:, :, :].rearrange("p k n -> p (k n)"), ALU.mult)\
                 .then_inc(*est.mid())
            dve.wait_ge(end_act, 8)
            V.scalar_tensor_tensor(out=VV, in0=SS1, scalar=1.0 / D, in1=SS0V, op0=ALU.mult, op1=ALU.add)\
             .then_inc(*est.mid())
            dve.wait_ge(*est.mine())
            for t in range(NT):
                V.scalar_tensor_tensor(out=TT[:, t:t + 1], in0=R0[:, t:t + 1], scalar=R0[:, t:t + 1],
                                       in1=VV[:, t:t + 1], op0=ALU.mult, op1=ALU.mult).then_inc(*est.mid())
            dve.wait_ge(*est.mine())
            V.tensor_scalar(TT, TT, -0.5, 1.5, ALU.mult, ALU.add).then_inc(*est.mid())
            dve.wait_ge(*est.mine())
            for t in range(NT):
                V.tensor_scalar(xn[:, t, :], xn[:, t, :], R0[:, t:t + 1], TT[:, t:t + 1], ALU.mult, ALU.mult)\
                 .then_inc(*est.mid())

        @block.tensor
        def _(pe):
            mm = nc.tensor.matmul

            def turn(o, i, n=P):
                return nc.tensor.transpose(o, i, ident[0:n, 0:n])

            pe.wait_ge(consts_made, 12)
            turn(bank["A0"][:, 0:P], gmaskT[:, :]).then_inc(pre_pe, 1)
            pe.wait_ge(pre_dve, 3)

            def turn_rows(b, j, src):
                for k in (0, 1):
                    for t in range(NT):
                        c = (2 * j + k) * P
                        ins = turn(bank[b][:, k * T + t * P:k * T + t * P + P], src[:, t, c:c + P])
                return ins

            def turn_scaled(b, j, src):
                for k in (0, 1):
                    for t in range(NT):
                        c = (2 * j + k) * P
                        ins = mm(bank[b][:, k * T + t * P:k * T + t * P + P], src[:, t, c:c + P], dg[t],
                                 start=True, stop=True)
                return ins

            for j, b in enumerate(TURN_BANKS):
                turn_scaled(b, j, xn).then_inc(pre_pe, 1)
            pe.wait_ge(pre_dve, 11)
            pe.wait_ge(x_landed, 16)

            with pe.Fori(0, DEPTH) as l:
                st = Steps(None, l)

                def three(o, lhi, llo, rhi, rlo, first, last, **kw):
                    mm(o, lhi, rhi, start=first, stop=False, **kw)
                    mm(o, lhi, rlo, start=False, stop=False, **kw)
                    return mm(o, llo, rhi, start=False, stop=last, **kw)

                def sources(key):
                    kind = key[0]
                    if kind in ("xk",):
                        return bT_hi, bT_lo, 4
                    if kind == "xv":
                        return bT_hi, bT_lo, 4 + 4 * key[1]
                    if kind == "glu":
                        return bT_hi, bT_lo, 0
                    if kind == "branch":
                        return {0: (hT_hi, hT_lo, 0), 1: (bT_hi, bT_lo, 4), 2: (bT_hi, bT_lo, 8)}[key[2]]
                    if kind == "wout":
                        return (bT_hi, bT_lo, 0) if key[1] % 2 == 0 else (hT_hi, hT_lo, 4)
                    if kind == "xo":
                        return bT_hi, bT_lo, 0
                    if kind == "down":
                        return bT_hi, bT_lo, 4 * (key[1] % 2)
                    return hT_hi, hT_lo, 4 * (key[1] % 2) if kind in ("sv", "dq", "dk", "dv") else 0

                def inputs(key):
                    if key == ("glu", 1):
                        return [(gelu_ready, KB)]
                    if key == ("branch", 0, 1):
                        return [freed("A3", ("sb_p", SB_HEADS - 2))]
                    if key == ("branch", 0, 2):
                        return [freed("X1", ("da_o", 1))]
                    if key == ("branch", 0, 0):
                        return [(glu_ready, 2)]
                    if key == ("wout", 0):
                        return [(mg_ready, 2)]
                    if key == ("wout", 1):
                        return [(mg_ready, 4)]
                    if key == ("xk", 0):
                        return [(mem_ready, KD)]
                    if key == ("xo", 0):
                        return [freed(stage_banks(("xa_p", h))[0], ("xa_p", h)) for h in (2, 3)]
                    if key[0] == "down" and key[2] == 0:
                        return [(hid_ready, 2 * key[1] + 2)]
                    return []

                def unit(u):
                    key = KEYS[u]
                    mat, kind, kt, cols, k0, c0 = UNITS[u]
                    banks = unit_banks(key)
                    pe.wait_ge(*st.at(hi_made, u + 1))
                    pe.wait_ge(*st.at(lo_made, u + 1))
                    pe.wait_ge(*st.at(lo_made_pool, u + 1))
                    for w in inputs(key):
                        pe.wait_ge(*st.at(*w))
                    if opens(key):
                        for b in banks:
                            pe.wait_ge(*st.at(*before(b, ("down",) if key[0] == "down" else key)))
                    hi, lo, s0 = sources(key)
                    wh, wl = wslot(w_hi[u % HL], u), wslot(w_lo[u % HL], u)
                    after_norm = {("u", 0): "mix", ("xq", 0): "cross", ("up", 0, 0): "mlp"}.get(key)
                    if after_norm:
                        for k in range(kt):
                            if k % 2 == 0:
                                pe.wait_ge(*st.at(h_ready, KD // 2 * NORMS.index(after_norm) + k // 2 + 1))
                            for ft in range(2):
                                c = slice(ft * P, ft * P + P)
                                ins = three(bank[banks[0]][:, ft * T:ft * T + T], wh[:, k, c], wl[:, k, c],
                                            hi[:, s0 + k, :], lo[:, s0 + k, :], k == 0 and ft == 0, k == kt - 1,
                                            skip_group_check=True)
                    elif kind == "T":
                        for ft in range(cols // P):
                            o = bank[banks[ft // 2]][:, (ft % 2) * T:(ft % 2) * T + T]
                            for k in range(kt):
                                c = slice(ft * P, ft * P + P)
                                ins = three(o, wh[:, k, c], wl[:, k, c], hi[:, s0 + k, :], lo[:, s0 + k, :],
                                            k == 0, k == kt - 1)
                    else:
                        for t in range(NT):
                            for k in range(kt):
                                c = slice(t * P, t * P + P)
                                ins = three(bank[banks[t]][:, :], hi[:, s0 + k, c], lo[:, s0 + k, c], wh[:, k, :],
                                            wl[:, k, :], opens(key) and k == 0, closes(key) and k == kt - 1)
                    ins.then_inc(*st.sig(unit_done))

                def stage(s):
                    kind = s[0]
                    if kind == "params":
                        pe.wait_ge(*st.at(prm_landed, 9))
                        pe.wait_ge(*st.at(prm_spread, 1))
                        pe.wait_ge(*st.at(*before("T0", s)))
                        turn(bank["T0"][:, 0:R_END], prm[0:R_END, :], R_END).then_inc(*st.sig(full["T0"]))
                    elif kind == "norm":
                        pe.wait_ge(*st.at(diag_ready, NT * (NORMS.index(s[1]) + 1)))
                        pe.wait_ge(*st.at(*before("A1", s)))
                        for t in range(NT):
                            ins = mm(bank["A1"][:, t * P:t * P + P], ones[:, :], dg[t], start=True, stop=True)
                        ins.then_inc(*st.sig(full["A1"]))
                    elif kind == "turn_x":
                        for t in range(NT):
                            pe.wait_ge(*st.at(*norm_input(s[1], s[2], t)))
                        for j, b in enumerate(stage_banks(s)):
                            pe.wait_ge(*st.at(*before(b, s)))
                            turn_rows(b, 2 * s[2] + j, x).then_inc(*st.sig(full[b]))
                    elif kind in ("ssm_bt", "ssm_ct"):
                        if kind == "ssm_bt":
                            pe.wait_ge(*st.at(b_ready, 1))
                        else:
                            pe.wait_ge(*st.at(mat_landed, 6))
                        src = bN if kind == "ssm_bt" else cN
                        for r, b in enumerate(stage_banks(s)):
                            pe.wait_ge(*st.at(*before(b, s)))
                            for k in range(4):
                                ins = turn(bank[b][:, k * P:k * P + P], src[:, r, k * P:k * P + P])
                            ins.then_inc(*st.sig(full[b]))
                    elif kind == "ssm_in":
                        i = s[1]
                        if i == 0:
                            pe.wait_ge(*st.at(*freed("A1", ("ssm_bt",))))
                            pe.wait_ge(*st.at(*freed("A3", ("ssm_ct",))))
                            pe.wait_ge(*st.at(*freed("T1", ("u", 1))))
                        for j, b in enumerate(("A0", "A1")):
                            pe.wait_ge(*st.at(*before(b, s)))
                            for r in range(2):
                                k, q = divmod(2 * i + j, 4)
                                ins = mm(bank[b][:, r * T:r * T + T], bt[32 * q:32 * q + 32, r, k, :],
                                         uT[32 * q:32 * q + 32, k, :], start=True, stop=True)
                            ins.then_inc(*st.sig(full[b]))
                    elif kind == "ssm_out":
                        i = s[1]
                        pe.wait_ge(*st.at(s_ready, i + 1))
                        pe.wait_ge(*st.at(s_im_ready, i + 1))
                        if i % 2 == 0:
                            pe.wait_ge(*st.at(*before("A2", s)))
                        for j in range(2):
                            k, q = divmod(2 * i + j, 4)
                            o = bank["A2"][32 * q:32 * q + 32, 0:T]
                            for r in range(2):
                                ins = mm(o, ct[:, r, k, 32 * q:32 * q + 32], s_re_im[:, r, j * T:j * T + T],
                                         start=(r == 0), stop=(r == 1))
                        ins.then_inc(*st.sig(s_used))
                    elif kind == "turn":
                        w = s[1]
                        pe.wait_ge(*st.at(rope_done, w + 1))
                        for j, b in enumerate(("X0", "X1")):
                            pe.wait_ge(*st.at(*before(b, s)))
                            turn_rows(b, j, dN[w]).then_inc(*st.sig(full[b]))
                    elif kind == "sb_s":
                        h = s[1]
                        r, c = slice(HD * (h % 2), HD * (h % 2) + HD), h // 2
                        if h == 0:
                            for b, i in (("T0", 0), ("T1", 1)):
                                pe.wait_ge(*st.at(*freed(b, ("sk", i))))
                        pe.wait_ge(*st.at(*before("X0", s)))
                        mm(bank["X0"][:, 0:T], qk[r, 4 + c, 0:P], qk[r, c, :], start=True, stop=True)
                        mm(bank["X0"][:, T:T + P], qk[r, 4 + c, P:T], qk[r, c, P:T], start=True, stop=True).then_inc(*st.sig(full["X0"]))
                    elif kind == "sb_u":
                        nl = nl_b[s[1] % 2]
                        pe.wait_ge(*st.at(nl_ready, s[1] + 1))
                        pe.wait_ge(*st.at(*before("X1", s)))
                        o = bank["X1"]
                        mm(o[:, 0:384], tri[:, :], nl, start=True, stop=True)
                        mm(o[:, P:T], ones[:, :], nl[:, T:384], start=False, stop=True, skip_group_check=True).then_inc(*st.sig(full["X1"]))
                    elif kind == "sb_p":
                        h = s[1]
                        w = z_b[h % 2]
                        pe.wait_ge(*st.at(w_ready, h + 1))
                        if h == 0:
                            pe.wait_ge(*st.at(*freed("T0", ("sv", 0))))
                            pe.wait_ge(*st.at(*freed("T1", ("sv", 0))))
                        if h % 2 == 0:
                            pe.wait_ge(*st.at(*before("A3", s)))
                        r = slice(HD * (h % 2), HD * (h % 2) + HD)
                        c = slice(HD * h, HD * h + HD)
                        mm(bank["A3"][r, 0:T], vN[:, 0, c], w[:, 0:T], start=True, stop=True, skip_group_check=True)
                        mm(bank["A3"][r, P:T], vN[:, 1, c], w[:, T:384], start=False, stop=True, skip_group_check=True)\
                            .then_inc(*st.sig(sbp_done))
                    elif kind == "da_s":
                        qt, h = divmod(s[1], DA_HEADS)
                        nk = P * (qt + 1)
                        for c, b in enumerate(("X0", "X1")):
                            pe.wait_ge(*st.at(*before(b, s)))
                            r = slice(HD * c, HD * c + HD)
                            mm(bank[b][:, 0:nk], dT[r, h, qt * P:qt * P + P], dT[r, 4 + h, 0:nk],
                                    start=True, stop=True).then_inc(*st.sig(full[b]))
                    elif kind == "da_t":
                        j = s[1]
                        pe.wait_ge(*st.at(dw_ready, j + 1))
                        pe.wait_ge(*st.at(*before("X1", s)))
                        for kb in range(j // DA_HEADS + 1):
                            ins = turn(bank["X1"][:, kb * P:kb * P + P], p_b[j % 2][:, 0, kb * P:kb * P + P])
                        ins.then_inc(*st.sig(full["X1"]))
                    elif kind == "da_p":
                        qt, h = divmod(s[1], DA_HEADS)
                        pe.wait_ge(*st.at(*freed("X1", ("da_t", s[1]))))
                        if s[1] == 0:
                            pe.wait_ge(*st.at(*freed("T0", ("dv", 0))))
                            pe.wait_ge(*st.at(*freed("T1", ("dv", 0))))
                        if h == 0:
                            pe.wait_ge(*st.at(*before("A3", s)))
                        for kb in range(qt + 1):
                            ins = mm(bank["A3"][:, h * P:h * P + P], pT_b[s[1] % 2][:, kb * P:kb * P + P],
                                     dv[:, kb, h * P:h * P + P], start=(kb == 0), stop=(kb == qt))
                        ins.then_inc(*st.sig(dap_done))
                    elif kind == "da_o":
                        pe.wait_ge(*st.at(on_ready, s[1] + 1))
                        pe.wait_ge(*st.at(*before("X1", s)))
                        for h in range(DA_HEADS):
                            ins = turn(bank["X1"][:, h * P:h * P + P], o_b[:, h * P:h * P + P])
                        ins.then_inc(*st.sig(full["X1"]))
                    elif kind == "xa_s":
                        h = s[1]
                        b = stage_banks(s)[0]
                        if h % 2 == 0:
                            pe.wait_ge(*st.at(*freed(f"T{h // 2}", ("xq", h // 2))))
                        pe.wait_ge(*st.at(*before(b, s)))
                        for qt in range(NT):
                            ins = mm(bank[b][:, qt * T:qt * T + T], qk[:, h, qt * P:qt * P + P], qk[:, 4 + h, :],
                                     start=True, stop=True)
                        ins.then_inc(*st.sig(full[b]))
                    elif kind == "xa_t":
                        h = s[1]
                        b = stage_banks(s)[0]
                        pe.wait_ge(*st.at(xw_ready, h + 1))
                        pe.wait_ge(*st.at(*before(b, s)))
                        for mt in range(2):
                            for qt in range(NT):
                                ins = turn(bank[b][:, mt * T + qt * P:mt * T + qt * P + P],
                                           e_b[h][:, qt, mt * P:mt * P + P])
                        ins.then_inc(*st.sig(full[b]))
                    elif kind == "xa_p":
                        h = s[1]
                        b = stage_banks(s)[0]
                        tb = stage_banks(("xa_t", h))[0]
                        pe.wait_ge(*st.at(*freed(tb, ("xa_t", h))))
                        if h == 0:
                            pe.wait_ge(*st.at(*freed("T0", ("xv", 0))))
                            pe.wait_ge(*st.at(*freed("T1", ("xv", 0))))
                        pe.wait_ge(*st.at(*before(b, s)))
                        for mt in range(2):
                            ins = mm(bank[b][:, 0:T], vN[:, mt, h * P:h * P + P], eT_b[h][:, mt, :],
                                     start=(mt == 0), stop=(mt == 1))
                        ins.then_inc(*st.sig(full[b]))

                for u in range(-1, NU):
                    if u >= 0:
                        unit(u)
                    for s in SIDE[u]:
                        stage(s)

    bad = [(s.name, s.made, s.per_layer) for s in signals if s.made != s.per_layer]
    assert not bad, bad


_INS = ["x", "mem", "positions", "norm_mix", "w_in", "ssm_lam_re", "ssm_lam_im", "ssm_log_dt", "ssm_b_re", "ssm_b_im",
        "ssm_c_re", "ssm_c_im", "ssm_d", "ssm_w_glu", "diff_lambda", "diff_subln", "w_branch", "w_out", "norm_cross",
        "norm_mem", "w_xq", "w_xkv", "w_xo", "norm_mlp", "w_up", "w_down", "norm_final"]


def kernel(**inputs):
    import numpy as _np
    import concourse.bacc as _bacc
    from concourse.bass_utils import run_bass_kernel_spmd as _run

    nc = _bacc.Bacc("TRN2", target_bir_lowering=False, num_devices=1)
    arrays, args = {}, {}
    for name in _INS:
        v = _np.ascontiguousarray(inputs[name])
        arrays[f"in_{name}"] = v
        args[name] = nc.dram_tensor(f"in_{name}", v.shape, mybir.dt.from_np(v.dtype), kind="ExternalInput").ap()
    out = nc.dram_tensor("out_0", (1, T, D), F32, kind="ExternalOutput").ap()
    hybrid_trunk(nc, args, out)
    r = _run(nc, [arrays], core_ids=[0])
    return r.results[0]["out_0"]
```
